# Optimizing a Trainium2 kernel written in Bass

```python
import jax, jax.numpy as jnp
from jax import lax
import numpy as np

D_MODEL = 1024
BATCH = 1
SEQ = 256
DEPTH = 1

N_MEM = 256
D_LRU = D_MODEL // 2
LRU_BLOCKS = 8
LRU_BLOCK_DIM = D_LRU // LRU_BLOCKS
CONV_WIDTH = 4
LRU_C = 8.0
D_ATTN = D_MODEL - D_LRU
ATTN_HEADS = 8
ATTN_HEAD_DIM = D_ATTN // ATTN_HEADS
MOBA_BLOCK = 256
MOBA_TOPK = 3
MOBA_Q_CHUNK = 16
D_IN = 2 * D_LRU + 3 * D_ATTN
CROSS_HEADS = 4
CROSS_HEAD_DIM = D_MODEL // CROSS_HEADS
PEER_KEYS = 128
PEER_EXPERTS = PEER_KEYS * PEER_KEYS
PEER_HEADS = 8
PEER_TOPK = 16
PEER_QDIM = 256
PEER_HALF = PEER_QDIM // 2
PEER_TOKEN_CHUNK = 128
PEER_V_SCALE = 0.5

EPS = 1e-6
NEG = -1e30

kernel_name = "hymba_rglru_moba_peer_block"

def rmsnorm(x, g):
    xf = x.astype(jnp.float32)
    y = xf * lax.rsqrt(jnp.mean(xf * xf, axis=-1, keepdims=True) + EPS)
    return (y * g.astype(jnp.float32)).astype(x.dtype)

def causal_depthwise_conv(x, w, b):
    y = lax.conv_general_dilated(
        x, w[:, None, :], window_strides=(1,), padding=[(CONV_WIDTH - 1, 0)],
        dimension_numbers=('NWC', 'WIO', 'NWC'), feature_group_count=x.shape[-1])
    return y + b

def rg_lru(x, wa, ba, wx, bx, lam):
    B, S, C = x.shape
    xb = x.reshape(B, S, LRU_BLOCKS, LRU_BLOCK_DIM)
    gate_r = jax.nn.sigmoid(jnp.einsum('bsnd,nde->bsne', xb, wa).reshape(B, S, C) + ba)
    gate_i = jax.nn.sigmoid(jnp.einsum('bsnd,nde->bsne', xb, wx).reshape(B, S, C) + bx)
    log_a = (-LRU_C * gate_r.astype(jnp.float32)) * jax.nn.softplus(-lam.astype(jnp.float32))
    a = jnp.exp(log_a)
    b = jnp.sqrt(-jnp.expm1(2.0 * log_a)) * (gate_i * x).astype(jnp.float32)

    def combine(left, right):
        a1, b1 = left
        a2, b2 = right
        return a1 * a2, a2 * b1 + b2

    _, h = lax.associative_scan(combine, (a, b), axis=1)
    return h.astype(x.dtype)

def moba_attention(q, k, v):
    B, S, H, Dh = q.shape
    nb = -(-S // MOBA_BLOCK)
    s_pad = nb * MOBA_BLOCK
    pad = [(0, 0), (0, s_pad - S), (0, 0), (0, 0)]
    q, k, v = (jnp.pad(t, pad).transpose(0, 2, 1, 3) for t in (q, k, v))
    scale = Dh ** -0.5
    k_blocks = k.reshape(B, H, nb, MOBA_BLOCK, Dh)
    v_blocks = v.reshape(B, H, nb, MOBA_BLOCK, Dh)
    k_mean = jnp.mean(k_blocks.astype(jnp.float32), axis=3)
    q_block = jnp.arange(s_pad) // MOBA_BLOCK
    gate = jnp.einsum('bhsd,bhnd->bhsn', q.astype(jnp.float32), k_mean)
    fully_past = jnp.arange(nb)[None, :] < q_block[:, None]
    gate = jnp.where(fully_past, gate, NEG)
    topk = min(MOBA_TOPK, nb)
    _, sel = lax.top_k(gate, topk)
    sel_valid = sel < q_block[:, None]
    gather_blocks = jax.vmap(jax.vmap(lambda blocks, idx: blocks[idx]))
    n_chunks = s_pad // MOBA_Q_CHUNK

    def chunk(c):
        start = c * MOBA_Q_CHUNK
        q_c = lax.dynamic_slice_in_dim(q, start, MOBA_Q_CHUNK, axis=2)
        sel_c = lax.dynamic_slice_in_dim(sel, start, MOBA_Q_CHUNK, axis=2)
        valid_c = lax.dynamic_slice_in_dim(sel_valid, start, MOBA_Q_CHUNK, axis=2)
        flat_sel = sel_c.reshape(B, H, MOBA_Q_CHUNK * topk)
        k_sel = gather_blocks(k_blocks, flat_sel).reshape(B, H, MOBA_Q_CHUNK, topk * MOBA_BLOCK, Dh)
        v_sel = gather_blocks(v_blocks, flat_sel).reshape(B, H, MOBA_Q_CHUNK, topk * MOBA_BLOCK, Dh)
        j = start // MOBA_BLOCK
        k_own = lax.dynamic_index_in_dim(k_blocks, j, axis=2, keepdims=False)
        v_own = lax.dynamic_index_in_dim(v_blocks, j, axis=2, keepdims=False)
        s_past = jnp.einsum('bhqd,bhqkd->bhqk', q_c, k_sel).astype(jnp.float32) * scale
        s_past = jnp.where(jnp.repeat(valid_c, MOBA_BLOCK, axis=-1), s_past, NEG)
        s_own = jnp.einsum('bhqd,bhkd->bhqk', q_c, k_own).astype(jnp.float32) * scale
        q_pos = start + jnp.arange(MOBA_Q_CHUNK)
        k_pos = j * MOBA_BLOCK + jnp.arange(MOBA_BLOCK)
        s_own = jnp.where(k_pos[None, :] <= q_pos[:, None], s_own, NEG)
        p = jax.nn.softmax(jnp.concatenate([s_past, s_own], axis=-1), axis=-1).astype(v.dtype)
        p_past, p_own = p[..., :topk * MOBA_BLOCK], p[..., topk * MOBA_BLOCK:]
        return (jnp.einsum('bhqk,bhqkd->bhqd', p_past, v_sel)
                + jnp.einsum('bhqk,bhkd->bhqd', p_own, v_own))

    out = lax.map(chunk, jnp.arange(n_chunks))
    out = out.transpose(1, 0, 3, 2, 4).reshape(B, s_pad, H, Dh)
    return out[:, :S]

def memory_cross_attention(xn, memn, w_q, w_k, w_v, w_o):
    B, S, _ = xn.shape
    M = memn.shape[1]
    q = (xn @ w_q).reshape(B, S, CROSS_HEADS, CROSS_HEAD_DIM)
    k = (memn @ w_k).reshape(B, M, CROSS_HEADS, CROSS_HEAD_DIM)
    v = (memn @ w_v).reshape(B, M, CROSS_HEADS, CROSS_HEAD_DIM)
    s = jnp.einsum('bshd,bmhd->bhsm', q, k).astype(jnp.float32) * CROSS_HEAD_DIM ** -0.5
    p = jax.nn.softmax(s, axis=-1).astype(v.dtype)
    o = jnp.einsum('bhsm,bmhd->bshd', p, v).reshape(B, S, D_MODEL)
    return o @ w_o

def peer_ffn(xn, w_q, sub_keys, u, v):
    B, S, D = xn.shape
    T = B * S
    t = xn.reshape(T, D)
    q = (t @ w_q).reshape(T, PEER_HEADS, 2, PEER_HALF)
    s = jnp.einsum('thpd,hpnd->thpn', q, sub_keys).astype(jnp.float32)
    s_top, i_top = lax.top_k(s, PEER_TOPK)
    cand_s = (s_top[:, :, 0, :, None] + s_top[:, :, 1, None, :]).reshape(T, PEER_HEADS, PEER_TOPK * PEER_TOPK)
    cand_i = (i_top[:, :, 0, :, None] * PEER_KEYS + i_top[:, :, 1, None, :]).reshape(T, PEER_HEADS, PEER_TOPK * PEER_TOPK)
    best_s, pos = lax.top_k(cand_s, PEER_TOPK)
    ids = jnp.take_along_axis(cand_i, pos, axis=-1).reshape(T, PEER_HEADS * PEER_TOPK)
    gates = jax.nn.softmax(best_s, axis=-1).reshape(T, PEER_HEADS * PEER_TOPK)
    n_chunks = T // PEER_TOKEN_CHUNK

    def chunk(args):
        x_c, ids_c, g_c = args
        act = jax.nn.gelu(jnp.einsum('td,ted->te', x_c, u[ids_c]), approximate=False)
        return jnp.einsum('te,ted->td', g_c.astype(x_c.dtype) * act, v[ids_c])

    y = lax.map(chunk, (t.reshape(n_chunks, PEER_TOKEN_CHUNK, D),
                        ids.reshape(n_chunks, PEER_TOKEN_CHUNK, -1),
                        gates.reshape(n_chunks, PEER_TOKEN_CHUNK, -1)))
    return y.reshape(B, S, D)

def hybrid_layer(x, mem, ln_mix_g, w_in, conv_w, conv_b, lru_wa, lru_ba, lru_wx, lru_bx,
                 lru_lambda, gn_lru_g, gn_attn_g, w_out, ln_cross_g, ln_mem_g, w_cq, w_ck,
                 w_cv, w_co, ln_ffn_g, peer_wq, peer_subkeys, peer_u, peer_v):
    B, S, _ = x.shape
    h = rmsnorm(x, ln_mix_g)
    proj = h @ w_in
    lru_x, lru_gate, q, k, v = jnp.split(
        proj, [D_LRU, 2 * D_LRU, 2 * D_LRU + D_ATTN, 2 * D_LRU + 2 * D_ATTN], axis=-1)
    lru_x = causal_depthwise_conv(lru_x, conv_w, conv_b)
    y_lru = rg_lru(lru_x, lru_wa, lru_ba, lru_wx, lru_bx, lru_lambda) * jax.nn.gelu(lru_gate, approximate=False)
    shp = (B, S, ATTN_HEADS, ATTN_HEAD_DIM)
    y_attn = moba_attention(q.reshape(shp), k.reshape(shp), v.reshape(shp)).reshape(B, S, D_ATTN)
    mixed = jnp.concatenate([rmsnorm(y_lru, gn_lru_g), rmsnorm(y_attn, gn_attn_g)], axis=-1)
    x = x + mixed @ w_out
    x = x + memory_cross_attention(rmsnorm(x, ln_cross_g), rmsnorm(mem, ln_mem_g), w_cq, w_ck, w_cv, w_co)
    x = x + peer_ffn(rmsnorm(x, ln_ffn_g), peer_wq, peer_subkeys, peer_u, peer_v)
    return x

def setup_inputs(seed: int = 0) -> dict:
    key = jax.random.key(seed)
    ks = jax.random.split(key, 32)

    def normal(k, shape, scale):
        return jax.random.normal(k, shape, jnp.float32) * scale

    def gain(k, shape):
        return 1.0 + normal(k, shape, 0.02)

    L = DEPTH
    u_a = jax.random.uniform(ks[8], (L, D_LRU), jnp.float32, minval=0.9, maxval=0.999)
    p_a = u_a ** (1.0 / LRU_C)
    lru_lambda = jnp.log(p_a) - jnp.log1p(-p_a)
    return {
        "x": normal(ks[0], (BATCH, SEQ, D_MODEL), 1.0),
        "mem": normal(ks[1], (BATCH, N_MEM, D_MODEL), 1.0),
        "ln_mix_g": gain(ks[2], (L, D_MODEL)),
        "w_in": normal(ks[3], (L, D_MODEL, D_IN), D_MODEL ** -0.5),
        "conv_w": normal(ks[4], (L, CONV_WIDTH, D_LRU), CONV_WIDTH ** -0.5),
        "conv_b": normal(ks[5], (L, D_LRU), 0.01),
        "lru_wa": normal(ks[6], (L, LRU_BLOCKS, LRU_BLOCK_DIM, LRU_BLOCK_DIM), LRU_BLOCK_DIM ** -0.5),
        "lru_ba": normal(ks[7], (L, D_LRU), 0.01),
        "lru_wx": normal(ks[9], (L, LRU_BLOCKS, LRU_BLOCK_DIM, LRU_BLOCK_DIM), LRU_BLOCK_DIM ** -0.5),
        "lru_bx": normal(ks[10], (L, D_LRU), 0.01),
        "lru_lambda": lru_lambda,
        "gn_lru_g": gain(ks[11], (L, D_LRU)),
        "gn_attn_g": gain(ks[12], (L, D_ATTN)),
        "w_out": normal(ks[13], (L, D_MODEL, D_MODEL), D_MODEL ** -0.5),
        "ln_cross_g": gain(ks[14], (L, D_MODEL)),
        "ln_mem_g": gain(ks[15], (L, D_MODEL)),
        "w_cq": normal(ks[16], (L, D_MODEL, D_MODEL), D_MODEL ** -0.5),
        "w_ck": normal(ks[17], (L, D_MODEL, D_MODEL), D_MODEL ** -0.5),
        "w_cv": normal(ks[18], (L, D_MODEL, D_MODEL), D_MODEL ** -0.5),
        "w_co": normal(ks[19], (L, D_MODEL, D_MODEL), D_MODEL ** -0.5),
        "ln_ffn_g": gain(ks[20], (L, D_MODEL)),
        "peer_wq": normal(ks[21], (L, D_MODEL, PEER_HEADS * PEER_QDIM), D_MODEL ** -0.5),
        "peer_subkeys": normal(ks[22], (L, PEER_HEADS, 2, PEER_KEYS, PEER_HALF), PEER_HALF ** -0.5),
        "peer_u": normal(ks[23], (L, PEER_EXPERTS, D_MODEL), D_MODEL ** -0.5),
        "peer_v": normal(ks[24], (L, PEER_EXPERTS, D_MODEL), PEER_V_SCALE),
        "ln_final_g": gain(ks[25], (D_MODEL,)),
    }

def reference(x, mem, ln_mix_g, w_in, conv_w, conv_b, lru_wa, lru_ba, lru_wx, lru_bx,
              lru_lambda, gn_lru_g, gn_attn_g, w_out, ln_cross_g, ln_mem_g, w_cq, w_ck,
              w_cv, w_co, ln_ffn_g, peer_wq, peer_subkeys, peer_u, peer_v, ln_final_g):
    for l in range(DEPTH):
        x = hybrid_layer(x, mem, ln_mix_g[l], w_in[l], conv_w[l], conv_b[l], lru_wa[l], lru_ba[l],
                         lru_wx[l], lru_bx[l], lru_lambda[l], gn_lru_g[l], gn_attn_g[l], w_out[l],
                         ln_cross_g[l], ln_mem_g[l], w_cq[l], w_ck[l], w_cv[l], w_co[l],
                         ln_ffn_g[l], peer_wq[l], peer_subkeys[l], peer_u[l], peer_v[l])
    return rmsnorm(x, ln_final_g)


_drawn_inputs = setup_inputs


def setup_inputs(seed=0):
    import zlib

    import numpy as np

    out = dict(_drawn_inputs(seed))
    spreads = {}
    factors = {'lru_ba': 8.0,
     'lru_bx': 6.934,
     'gn_lru_g': 2.789,
     'ln_cross_g': 7.406,
     'ln_mem_g': 6.05,
     'ln_final_g': 7.841,
     'ln_ffn_g': 8.0}
    for name, (base, spread) in spreads.items():
        noise = np.random.default_rng([zlib.crc32(name.encode()), seed]).standard_normal(out[name].shape)
        drawn = base * np.exp(spread * noise) if base else spread * noise
        out[name] = __import__('jax').numpy.asarray(drawn.astype(out[name].dtype))
    for name, factor in factors.items():
        out[name] = (out[name] * factor).astype(out[name].dtype)
    return out
```

```python
from contextlib import ExitStack

import concourse.bass as bass
from concourse import mybir

F32 = mybir.dt.float32
F32R = mybir.dt.float32r
U32 = mybir.dt.uint32
ALU = mybir.AluOpType
ACT = mybir.ActivationFunctionType
X = mybir.AxisListType.X
ds = bass.ds

P = 128
T, D = 256, 1024
TT, DC = T // P, D // P
LC = 4
HEADS, DH = 8, 64
CHEADS, CDH = 4, 256
PH, TOPK, KEYS = 8, 16, 128
CONV = 4
EPS = 1e-6
NEG = -1e30
LOWEST = -3.0e38
WCOL = 256

PAR = {}
_at = 0
for _name, _n in (("ln_mix", DC), ("ln_mem", DC), ("ln_cross", DC), ("ln_ffn", DC), ("gn_lru", LC), ("gn_attn", LC),
                  ("conv_w", CONV * LC), ("conv_b", LC), ("ba", LC), ("bx", LC), ("lam", LC)):
    PAR[_name] = (_at, _n)
    _at += _n
NPAR = _at

UNITS = ([("w_in", WCOL * i, "cols") for i in range(8)] + [("w_in", WCOL * i, "rows") for i in range(8, 10)]
         + [("w_ck", WCOL * i, "cols") for i in range(4)] + [("w_cv", WCOL * i, "rows") for i in range(4)]
         + [("w_out", WCOL * i, "groups") for i in range(4)]
         + [("w_cq", WCOL * i, "cols") for i in range(4)] + [("w_co", WCOL * i, "rows") for i in range(4)]
         + [("w_pq", WCOL * i, "cols") for i in range(8)])
U_LRU, U_GATE, U_Q, U_K, U_V, U_CK, U_CV, U_OUT, U_CQ, U_CO, U_PQ = 0, 2, 4, 6, 8, 10, 14, 18, 22, 26, 30
NU = len(UNITS)
WRAW = 4
DVE_EVAC = set(range(U_OUT, U_CQ)) | set(range(U_CO, U_PQ))

JPB = 8
GRP = 4


def build(nc, x, mem, par, wa, wx, w, keys_t, u_t, v, g_final, out):
    ctx = ExitStack()
    with ctx:
        base = 16512

        def at(name, off, shape, dt=F32):
            return nc.alloc_sbuf_tensor_at(name, [P] + shape, dt, offset=base + off)

        def sem(name):
            return ctx.enter_context(nc.semaphore(name))

        K = 1024
        act_w = at("act_w", 0, [KEYS, T])
        xr = at("xr", 128 * K, [TT, D])
        xt = at("xt", 136 * K, [DC, 2, T], F32R)
        raw = at("raw", 152 * K, [2, 2, D])
        hl = at("hl", 168 * K, [2, 2, D], F32R)
        gfin = at("gfin", 136 * K, [D])
        fin = at("fin", 140 * K, [TT, D])
        m = 184 * K
        ident = at("ident", m, [P]); m += 512
        iota = at("iota", m, [P]); m += 512
        pars = at("pars", m, [NPAR]); m += 288
        ones = at("ones", m, [8]); m += 32
        stat = at("stat", m, [96]); m += 384
        kt3 = at("kt3", m, [3, T]); m += 3 * K
        krow = at("krow", m, [3, TT, P]); m += 3 * K
        oh_at = m
        oh_i = at("oh_i", m, [2, GRP, P]); m += 4 * K
        oh_j = at("oh_j", m, [2, GRP, P]); m += 4 * K
        tmp_at = m
        whl = at("whl", m, [2, 2, T], F32R)
        cand = at("cand", m, [256])
        candw = at("candw", m + K, [256])
        rwork = at("rwork", m + 2 * K, [P])
        eq = at("eq", m + 2 * K + 512, [2, TOPK, TOPK])
        topv = at("topv", m + 4 * K + 512, [3, TOPK])
        topi = at("topi", m + 4 * K + 704, [3, TOPK], U32)
        posu = at("posu", m + 4 * K + 896, [2, TOPK], U32)
        posf = at("posf", m + 4 * K + 1024, [2, TOPK])
        topf = at("topf", m + 4 * K + 1152, [2, TOPK])
        m += 5 * K + 256
        mask = at("mask", m, [3 * P]); m += 1536
        assert base + m <= 229344
        wraw = at("wraw", 0, [WRAW, DC, WCOL])
        wsp = at("wsp", 32 * K, [2, 2, DC, WCOL], F32R)
        mr = at("mr", 64 * K, [TT, D])
        v_sb = at("v_sb", 64 * K, [TT, 512])
        ya = at("ya", 68 * K, [LC, T])
        memt = at("memt", 72 * K, [DC, 2, T], F32R)
        qct = at("qct", 72 * K, [DC, T])
        keys = at("keys", 80 * K, [2 * PH, KEYS])
        xs = at("xs", 88 * K, [TT, D])
        pbuf = at("pbuf", 88 * K, [2, 512])
        ptr = at("ptr", 92 * K, [2, 512])
        mixt = at("mixt", 96 * K, [DC, 2, T], F32R)
        oct_ = at("oct", 96 * K, [DC, 2, T], F32R)
        qpt = at("qpt", 96 * K, [2 * PH, T])
        kct = at("kct", 112 * K, [DC, T])
        bd = at("bd", 120 * K, [2, LC, P])
        vc = at("vc", 120 * K, [TT, D])
        srow = at("srow", 112 * K, [TT * PH, 2, KEYS])
        cx = at("cx", oh_at, [LC, T + CONV - 1])
        lru = at("lru", 152 * K, [8, LC, T])
        cv_, r_, i_, a_, th_, gel = (lru[:, k] for k in range(6))
        qt, ktt = lru[:, 6], lru[:, 7]

        def flat(ap):
            return ap.rearrange("p a b -> p (a b)")

        bank = [ctx.enter_context(nc.psum_tensor(f"bank{i}", [P, 512], F32)) for i in range(4, 8)]
        acc = ctx.enter_context(nc.psum_tensor("acc", [P, 4, 512], F32))

        SS, RS = 0, 16
        ND = 32
        SP = 48
        GS = 72
        s_par, s_x, s_mem, s_bd, s_keys, s_gf, s_out = (sem(n) for n in (
            "s_par", "s_x", "s_mem", "s_bd", "s_keys", "s_gf", "s_out"))
        s_wr = [sem(f"s_wraw{i}") for i in range(WRAW)]
        s_wh, s_wl, s_wmm, s_weva, s_wevd = (sem(n) for n in ("s_w_high", "s_w_low", "s_w_mm", "s_w_evac_act", "s_w_evac_dve"))
        s_const = sem("s_const")
        s_sq, s_var, s_std, s_xs, s_tr, s_th, s_tl = (sem(n) for n in (
            "s_squares", "s_variance", "s_deviation", "s_scaled", "s_transposed", "s_t_high", "s_t_low"))
        s_pool, s_dve, s_act = sem("s_pool_chain"), sem("s_dve_chain"), sem("s_act_chain")
        s_spe, s_spc = sem("s_softplus_exp"), sem("s_softplus_done")
        s_cv, s_lg, s_sg, s_at, s_b2, s_sqr, s_y = (sem(n) for n in (
            "s_conv", "s_lru_gate_mm", "s_lru_sigmoid", "s_lru_a_tanh", "s_lru_1ma2", "s_lru_sqrt", "s_lru_y"))
        s_gss, s_gmm, s_gh, s_gl = (sem(n) for n in ("s_group_squares", "s_group_sums", "s_group_high", "s_group_low"))
        s_sc, s_mx, s_ex, s_pn, s_pt, s_pe, s_pv, s_pve = (sem(n) for n in (
            "s_scores", "s_att_max", "s_att_exp", "s_att_probs", "s_att_transposed", "s_att_probs_t", "s_att_pv", "s_att_out"))
        s_cl = sem("s_cross_low")
        s_ks, s_ke, s_rt, s_ge, s_gr, s_ktr, s_kte = (sem(n) for n in (
            "s_key_scores", "s_key_rows", "s_routed", "s_gate_exp", "s_gates", "s_key_transposed", "s_key_cols"))
        s_raw = [sem(f"s_raw{i}") for i in range(2)]
        s_uh, s_ul, s_um, s_ua = (sem(n) for n in ("s_u_high", "s_u_low", "s_u_mm", "s_u_gelu"))
        s_oi, s_oj, s_gm, s_gw = (sem(n) for n in ("s_onehot_i", "s_onehot_j", "s_route_mm", "s_route_mul"))
        s_vh, s_vl, s_Wh, s_Wl, s_vm = (sem(n) for n in ("s_v_high", "s_v_low", "s_a_high", "s_a_low", "s_v_mm"))
        s_fs, s_fv, s_fd, s_fin = (sem(n) for n in ("s_fin_squares", "s_fin_var", "s_fin_dev", "s_fin"))

        def pcol(name, c, n=1):
            o = PAR[name][0] + c
            return pars[:, o:o + n]

        def rows(ap):
            return ap.rearrange("(t p) d -> p t d", p=P)

        wd = {n: a.rearrange("(c p) n -> p c n", p=P) for n, a in w.items()}
        vd = v.rearrange("(i q j) d -> q i j d", i=KEYS, j=2)
        SCB, TRB, OUB = 0, 2, 3

        def wevac(eng, u):
            if u in DVE_EVAC:
                eng.wait_ge(s_wevd, sum(1 for k in DVE_EVAC if k <= u))
            else:
                eng.wait_ge(s_weva, sum(1 for k in range(u + 1) if k not in DVE_EVAC))

        block = ctx.enter_context(nc.Block())

        @block.sync
        def _(sp):
            sp.dma_start(xr[:], rows(x)).then_inc(s_x, 16)
            sp.dma_start(pars[:], par).then_inc(s_par, 16)

            def unit(u):
                name, c0, _ = UNITS[u]
                if u >= WRAW:
                    sp.wait_ge(s_wl, u - WRAW + 1)
                sp.dma_start(wraw[:, u % WRAW], wd[name][:, :, c0:c0 + WCOL]).then_inc(s_wr[u % WRAW], 16)

            for u in range(2):
                unit(u)
            sp.dma_start(mr[:], rows(mem)).then_inc(s_mem, 16)
            for u in range(2, WRAW):
                unit(u)
            sp.wait_ge(s_const, 7)
            for k, src in enumerate((wa, wx)):
                for half in range(2):
                    q = slice(64 * half, 64 * half + 64)
                    sp.dma_start(bd[q, k, :, q], src[half::2].rearrange("m d e -> d m e")).then_inc(s_bd, 16)
            for u in range(WRAW, NU):
                unit(u)
                if u == U_PQ + 4:
                    sp.dma_start(keys[:], keys_t).then_inc(s_keys, 16)

            sp.wait_ge(s_pv, 8 + 4)
            for q in range(2):
                sp.dma_start(raw[:, q], u_t[q]).then_inc(s_raw[q], 16)
            with sp.Fori(1, KEYS // 4) as it:
                for q in range(2):
                    sp.wait_ge(s_ul, it * 4 - 4 + 2 * q + 2)
                    sp.dma_start(raw[:, q], u_t[ds(it * 2 + q, 1)].rearrange("o p j d -> (o p) j d")).then_inc(s_raw[q], 16)
            for q in range(2):
                sp.wait_ge(s_ul, KEYS - 4 + 2 * q + 2)
                sp.dma_start(raw[:, q], vd[q]).then_inc(s_raw[q], 16)
            sp.wait_ge(s_um, KEYS)
            sp.dma_start(gfin[:], g_final.rearrange("(o d) -> o d", o=1).broadcast_to([P, D])).then_inc(s_gf, 16)
            with sp.Fori(1, KEYS // 4) as it:
                for q in range(2):
                    sp.wait_ge(s_vl, it * 4 - 4 + 2 * q + 2)
                    sp.dma_start(raw[:, q], vd[ds(it * 2 + q, 1)].rearrange("o i j d -> (o i) j d")).then_inc(s_raw[q], 16)
            for t in range(TT):
                sp.wait_ge(s_fin, t + 1)
                sp.dma_start(out[P * t:P * t + P, :], fin[:, t]).then_inc(s_out, 16)
            sp.wait_ge(s_out, 16 * TT)

        @block.gpsimd
        def _(pool):
            nc.gpsimd.memset(bd[:].rearrange("p a b c -> p (a b c)"), 0.0).then_inc(s_const, 1)
            nc.gpsimd.memset(ident[:], 0.0).then_inc(s_pool, 1)
            nc.gpsimd.memset(mask[:], 0.0).then_inc(s_pool, 1)
            pool.wait_ge(s_pool, 2)
            nc.gpsimd.affine_select(out=ident[:], in_=ident[:], compare_op=ALU.not_equal, fill=1.0, base=0,
                                    pattern=[[-1, P]], channel_multiplier=1).then_inc(s_const, 1)
            nc.gpsimd.affine_select(out=mask[:, 0:P], in_=mask[:, 0:P], compare_op=ALU.is_ge, fill=NEG, base=0,
                                    pattern=[[-1, P]], channel_multiplier=1).then_inc(s_const, 1)
            nc.gpsimd.affine_select(out=mask[:, P:3 * P], in_=mask[:, P:3 * P], compare_op=ALU.is_ge, fill=NEG, base=P,
                                    pattern=[[-1, 2 * P]], channel_multiplier=1).then_inc(s_const, 1)
            nc.gpsimd.iota(iota[:], pattern=[[1, P]], base=0, channel_multiplier=0,
                           allow_small_or_imprecise_dtypes=True).then_inc(s_const, 1)
            nc.gpsimd.memset(ones[:], 1.0).then_inc(s_const, 1)
            nc.gpsimd.memset(cx[:, :, 0:CONV - 1], 0.0).then_inc(s_const, 1)
            pool.wait_ge(s_const, 7)
            pool.wait_ge(s_kte, 1)

            for g in range(T // GRP):
                if g >= 2:
                    pool.wait_ge(s_gm, g - 1)
                for k in range(GRP):
                    t = GRP * g + k
                    last = nc.gpsimd.tensor_scalar(oh_j[:, g % 2, k, :], iota[:], kt3[:, 1, t:t + 1], None, ALU.is_equal)
                last.then_inc(s_oj, 1)

        @block.scalar
        def _(act):
            chain = [0]

            def link(ins):
                chain[0] += 1
                ins.then_inc(s_act, 1)
                act.wait_ge(s_act, chain[0])

            def w_high(u):
                act.wait_ge(s_wr[u % WRAW], 16 * (u // WRAW + 1))
                if u >= 2:
                    act.wait_ge(s_wmm, u - 1)
                nc.scalar.activation(wsp[:, u % 2, 0], wraw[:, u % WRAW], ACT.Copy).then_inc(s_wh, 1)

            def unit(u, dst=None):
                if u + 2 < NU:
                    w_high(u + 2)
                if u in DVE_EVAC:
                    return
                act.wait_ge(s_wmm, u + 1)
                for k in range(2):
                    last = nc.scalar.activation(dst(k), acc[:, 2 * (u % 2) + k, 0:WCOL], ACT.Copy)
                last.then_inc(s_weva, 1)

            def squares(n, src, junk):
                for t in range(TT):
                    last = nc.scalar.activation(junk[:, t], src[:, t], ACT.Square, accum_out=stat[:, SS + 2 * n + t:SS + 2 * n + t + 1])
                last.then_inc(s_sq, 1)

            def deviation(n, k):
                act.wait_ge(s_var, k)
                nc.scalar.activation(stat[:, RS + 2 * n:RS + 2 * n + 2], stat[:, SS + 2 * n:SS + 2 * n + 2], ACT.Sqrt).then_inc(s_std, 1)

            def t_high(k, gain, dst):
                for c in range(DC):
                    if c % 2 == 0:
                        act.wait_ge(s_tr, 4 * k + c // 2 + 1)
                    nc.scalar.activation(dst[:, c, 0], bank[c // 2][:, T * (c % 2):T * (c % 2) + T], ACT.Copy,
                                         scale=pcol(gain, c)).then_inc(s_th, 1)

            act.wait_ge(s_x, 16)
            squares(0, xr, xs)
            act.wait_ge(s_mem, 16)
            squares(1, mr, kct[:].rearrange("p (t c) n -> p t (c n)", t=TT))
            deviation(0, 1)
            deviation(1, 2)
            act.wait_ge(s_spe, 1)
            nc.scalar.activation(stat[:, SP + 4:SP + 8], stat[:, SP:SP + 4], ACT.Exp, scale=-1.0).then_inc(s_spc, 1)
            w_high(0)
            w_high(1)
            act.wait_ge(s_par, 16)
            t_high(0, "ln_mix", xt)
            act.wait_ge(s_const, 7)
            for u in (0, 1):
                unit(u, lambda k: cx[:, 2 * u + k, CONV - 1:])
            t_high(1, "ln_mem", memt)
            for u in (2, 3):
                unit(u, lambda k: gel[:, 2 * (u - U_GATE) + k])
            for mch in range(LC):
                act.wait_ge(s_lg, mch + 1)
                nc.scalar.activation(r_[:, mch], bank[mch][:, 0:T], ACT.Sigmoid, bias=pcol("ba", mch))
                nc.scalar.activation(i_[:, mch], bank[mch][:, T:2 * T], ACT.Sigmoid, bias=pcol("bx", mch)).then_inc(s_sg, 1)
            for u in (4, 5):
                unit(u, lambda k: qt[:, 2 * (u - U_Q) + k])
            act.wait_ge(s_spc, 2)
            act.wait_ge(s_sg, LC)
            for mch in range(LC):
                nc.scalar.activation(a_[:, mch], r_[:, mch], ACT.Exp, scale=stat[:, SP + 20 + mch:SP + 21 + mch])
                last = nc.scalar.activation(th_[:, mch], r_[:, mch], ACT.Tanh, scale=stat[:, SP + 20 + mch:SP + 21 + mch])
            last.then_inc(s_at, 1)
            for u in (6, 7):
                unit(u, lambda k: ktt[:, 2 * (u - U_K) + k])
            act.wait_ge(s_weva, 4)
            nc.scalar.activation(gel[:], gel[:], ACT.Gelu).then_inc(s_at, 1)
            act.wait_ge(s_b2, 1)
            nc.scalar.activation(th_[:], th_[:], ACT.Sqrt, scale=-1.0).then_inc(s_sqr, 1)
            for u in (8, 9):
                unit(u, lambda k: v_sb[:, k, WCOL * (u - U_V):WCOL * (u - U_V) + WCOL])
            act.wait_ge(s_y, 1)
            nc.scalar.activation(r_[:], a_[:], ACT.Square).then_inc(s_gss, 1)

            def softmax_exp(n, scale, widths, src):
                slot = n % 2
                st = ND + 6 * slot
                act.wait_ge(s_mx, n + 1)
                o = 0
                for t, wdt in enumerate(widths):
                    last = nc.scalar.activation(pbuf[:, slot, o:o + wdt], src[:, o:o + wdt], ACT.Exp, scale=scale,
                                                bias=stat[:, st + t:st + t + 1], accum_out=stat[:, st + 2 + t:st + 3 + t])
                    o += wdt
                last.then_inc(s_ex, 1)

            def probs_t(n, cols):
                slot = n % 2
                act.wait_ge(s_pt, n + 1)
                if n >= 2:
                    act.wait_ge(s_pv, n - 1)
                nc.scalar.activation(ptr[:, slot, 0:cols], bank[TRB][:, 0:cols], ACT.Copy).then_inc(s_pe, 1)

            for h in range(HEADS):
                softmax_exp(h, 1.0, (P, 2 * P), pbuf[:, h % 2])
                u = U_CK + h
                if u < U_CV:
                    unit(u, lambda k: kct[:, 2 * (u - U_CK) + k])
                else:
                    unit(u, lambda k: vc[:, k, WCOL * (u - U_CV):WCOL * (u - U_CV) + WCOL])
                probs_t(h, 3 * P)
            act.wait_ge(s_pve, HEADS)
            nc.scalar.activation(i_[:], ya[:], ACT.Square).then_inc(s_gss, 1)
            for c in range(DC):
                src, gain = (a_, "gn_lru") if c < LC else (ya, "gn_attn")
                nc.scalar.activation(mixt[:, c, 0], src[:, c % LC], ACT.Copy, scale=pcol(gain, c % LC)).then_inc(s_gh, 1)
            act.wait_ge(s_var, 3)
            nc.scalar.activation(stat[:, RS + 12:RS + 16], stat[:, SS + 12:SS + 16], ACT.Sqrt).then_inc(s_std, 1)
            for u in range(U_OUT, U_CQ):
                unit(u)
            act.wait_ge(s_wevd, 4)
            squares(2, xr, xs)
            deviation(2, 4)
            t_high(2, "ln_cross", xt)
            for u in range(U_CQ, U_CO):
                unit(u, lambda k: qct[:, 2 * (u - U_CQ) + k])
            for h in range(CHEADS):
                n = HEADS + h
                softmax_exp(n, CDH ** -0.5, (T, T), bank[SCB + n % 2])
                probs_t(n, 2 * T)
                act.wait_ge(s_pv, n + 1)
                nc.scalar.activation(oct_[:, 2 * h:2 * h + 2, 0], bank[OUB][:].rearrange("p (c t) -> p c t", c=2),
                                     ACT.Copy).then_inc(s_gh, 1)
            for u in range(U_CO, U_PQ):
                unit(u)
            act.wait_ge(s_wevd, 8)
            squares(3, xr, xs)
            deviation(3, 5)
            t_high(3, "ln_ffn", xt)
            for u in range(U_PQ, NU):
                unit(u, lambda k: qpt[:, 2 * (u - U_PQ) + k])
            sr = srow[:].rearrange("p (t h) a k -> p t (h a k)", t=TT)
            for n in range(8):
                act.wait_ge(s_ks, n + 1)
                nc.scalar.activation(sr[:, n // 4, 512 * (n % 4):512 * (n % 4) + 512], bank[n % 4][:], ACT.Copy).then_inc(s_ke, 1)

            def split_high(k, landed, free, ready):
                if landed is not None:
                    act.wait_ge(s_raw[k // 2], landed)
                if free is not None:
                    act.wait_ge(*free)
                nc.scalar.activation(hl[:, k % 2, 0], raw[:, k // 2, k % 2], ACT.Copy).then_inc(ready, 1)

            def gelu(j, k):
                act.wait_ge(s_um, j + 1)
                nc.scalar.activation(act_w[:, ds(j, 1)].rearrange("p o t -> p (o t)"), bank[k % 4][:, 0:T], ACT.Gelu).then_inc(s_ua, 1)

            act.wait_ge(s_pv, 12)
            split_high(0, 16, None, s_uh)
            split_high(1, None, None, s_uh)

            def u_pass(it, last):
                for jj in range(JPB):
                    j = it * JPB + jj
                    k = jj + 2
                    if not (last and k >= JPB):
                        split_high(k % 4, (it * 2 + k // 4 + 1) * 16 if k % 2 == 0 else None, (s_um, j + 1), s_uh)
                    if jj == JPB - 1:
                        act.wait_ge(s_rt, it + 1)
                    gelu(j, jj)

            with act.Fori(0, KEYS // JPB - 1) as it:
                u_pass(it, False)
            u_pass(KEYS // JPB - 1, True)

            act.wait_ge(s_rt, TT * PH)
            nc.scalar.activation(krow[:, 2], krow[:, 2], ACT.Exp).then_inc(s_ge, 1)
            act.wait_ge(s_ktr, 1)
            link(nc.scalar.activation(flat(kt3[:, 0:2]), bank[0][:], ACT.Copy))
            nc.scalar.activation(kt3[:, 2], bank[1][:, 0:T], ACT.Copy).then_inc(s_kte, 1)

            base16 = 16 * (KEYS // 4)
            split_high(0, base16 + 16, (s_um, KEYS), s_vh)
            split_high(1, None, None, s_vh)

            def a_high(j, slot):
                nc.scalar.activation(whl[:, slot, 0], act_w[:, ds(j, 1)].rearrange("p o t -> p (o t)"), ACT.Copy).then_inc(s_Wh, 1)

            act.wait_ge(s_gw, T // GRP)
            a_high(0, 0)
            a_high(1, 1)

            def v_pass(it, last):
                for jj in range(4):
                    k = jj + 2
                    if last and k >= 4:
                        continue
                    j = it * 4 + jj
                    split_high(k % 4, (it + k // 4 + 1) * 16 + base16 if k % 2 == 0 else None, (s_vm, j + 1), s_vh)
                    a_high(j + 2, jj % 2)

            with act.Fori(0, KEYS // 4 - 1) as it:
                v_pass(it, False)
            v_pass(KEYS // 4 - 1, True)
            act.wait_ge(s_vm, KEYS)
            act.wait_ge(s_gf, 16)
            for t in range(TT):
                nc.scalar.activation(fin[:, t].rearrange("p (a n) -> p a n", a=2), acc[:, 2 * t:2 * t + 2, :], ACT.Square,
                                     accum_out=stat[:, SS + t:SS + t + 1]).then_inc(s_fs, 1)
            act.wait_ge(s_fv, 1)
            nc.scalar.activation(stat[:, RS:RS + 2], stat[:, SS:SS + 2], ACT.Sqrt).then_inc(s_fd, 1)

        @block.vector
        def _(dve):
            V = nc.vector
            chain = [0]

            def link(ins):
                chain[0] += 1
                ins.then_inc(s_dve, 1)
                dve.wait_ge(s_dve, chain[0])

            def w_low(u):
                dve.wait_ge(s_wh, u + 1)
                V.tensor_tensor(wsp[:, u % 2, 1], wraw[:, u % WRAW], wsp[:, u % 2, 0].bitcast(F32), ALU.subtract).then_inc(s_wl, 1)

            def unit(u):
                if u + 2 < NU:
                    w_low(u + 2)

            def variance(n, k, cols=2, width=D):
                dve.wait_ge(s_sq, k)
                V.tensor_scalar(stat[:, SS + 2 * n:SS + 2 * n + cols], stat[:, SS + 2 * n:SS + 2 * n + cols],
                                1.0 / width, EPS, ALU.mult, ALU.add).then_inc(s_var, 1)

            def scaled(n, k, src, dst):
                dve.wait_ge(s_std, k)
                rs = stat[:, RS + 2 * n:RS + 2 * n + 2]
                link(V.reciprocal(rs, rs))
                for t in range(TT):
                    last = V.tensor_scalar(dst[:, t], src[:, t], rs[:, t:t + 1], None, ALU.mult)
                last.then_inc(s_xs, 1)

            def t_low(k, gain, dst):
                for c in range(DC):
                    dve.wait_ge(s_th, DC * k + c + 2 - c % 2)
                    V.scalar_tensor_tensor(dst[:, c, 1], bank[c // 2][:, T * (c % 2):T * (c % 2) + T], pcol(gain, c),
                                           dst[:, c, 0].bitcast(F32), ALU.mult, ALU.subtract).then_inc(s_tl, 1)

            dve.wait_ge(s_par, 16)
            lam = pcol("lam", 0, LC)
            c4 = lambda k: stat[:, SP + 4 * k:SP + 4 * k + 4]
            V.scalar_tensor_tensor(c4(0), lam, -1.0, lam, ALU.mult, ALU.max).then_inc(s_spe, 1)
            variance(0, 1)
            variance(1, 2)
            scaled(0, 1, xr, xs)
            scaled(1, 2, mr, mr)
            dve.wait_ge(s_spc, 1)
            e, z, z2, q, sp8 = c4(1), c4(2), c4(3), c4(4), c4(5)
            link(V.tensor_scalar(z, e, 2.0, None, ALU.add))
            link(V.reciprocal(z, z))
            link(V.tensor_tensor(z, z, e, ALU.mult))
            link(V.tensor_tensor(z2, z, z, ALU.mult))
            link(V.tensor_scalar(q, z2, 1.0 / 17, None, ALU.mult))
            for n in (15, 13, 11, 9, 7, 5, 3):
                link(V.scalar_tensor_tensor(q, q, 1.0 / n, z2, ALU.add, ALU.mult))
            link(V.scalar_tensor_tensor(q, q, 1.0, z, ALU.add, ALU.mult))
            link(V.tensor_scalar(z, lam, -1.0, 0.0, ALU.mult, ALU.max))
            link(V.scalar_tensor_tensor(sp8, q, 2.0, z, ALU.mult, ALU.add))
            V.tensor_scalar(sp8, sp8, -8.0, None, ALU.mult).then_inc(s_spc, 1)
            w_low(0)
            w_low(1)
            t_low(0, "ln_mix", xt)
            unit(0)
            unit(1)
            dve.wait_ge(s_weva, 2)
            for s in range(CONV):
                for mch in range(LC):
                    wcol = pcol("conv_w", LC * s + mch)
                    if s:
                        V.scalar_tensor_tensor(cv_[:, mch], cx[:, mch, s:s + T], wcol, cv_[:, mch], ALU.mult, ALU.add).then_inc(s_cv, 1)
                    else:
                        V.tensor_scalar(cv_[:, mch], cx[:, mch, 0:T], wcol, pcol("conv_b", mch), ALU.mult, ALU.add).then_inc(s_cv, 1)
                dve.wait_ge(s_cv, LC * (s + 1))
            t_low(1, "ln_mem", memt)
            for u in range(2, 6):
                unit(u)
            dve.wait_ge(s_sg, LC)
            link(V.tensor_tensor(i_[:], i_[:], cv_[:], ALU.mult))
            dve.wait_ge(s_at, 1)
            link(V.tensor_tensor(r_[:], a_[:], a_[:], ALU.mult))
            V.scalar_tensor_tensor(th_[:], r_[:], 1.0, th_[:], ALU.add, ALU.mult).then_inc(s_b2, 1)
            unit(6)
            unit(7)
            dve.wait_ge(s_sqr, 1)
            link(V.tensor_tensor(i_[:], i_[:], th_[:], ALU.mult))
            for mch in range(LC):
                last = V.tensor_tensor_scan(r_[:, mch], a_[:, mch], i_[:, mch], 0.0, ALU.mult, ALU.add)
            link(last)
            dve.wait_ge(s_at, 2)
            V.tensor_tensor(a_[:], r_[:], gel[:], ALU.mult).then_inc(s_y, 1)
            unit(8)
            unit(9)

            def normalise(n, widths):
                slot = n % 2
                st = ND + 6 * slot
                dve.wait_ge(s_ex, n + 1)
                link(V.reciprocal(stat[:, st + 4:st + 6], stat[:, st + 2:st + 4]))
                o = 0
                for t, wdt in enumerate(widths):
                    last = V.tensor_scalar(pbuf[:, slot, o:o + wdt], pbuf[:, slot, o:o + wdt], stat[:, st + 4 + t:st + 5 + t],
                                           None, ALU.mult)
                    o += wdt
                last.then_inc(s_pn, 1)

            def masked_max(h):
                slot = h % 2
                dve.wait_ge(s_sc, h + 1)
                if h >= 2:
                    dve.wait_ge(s_pt, h - 1)
                link(V.scalar_tensor_tensor(pbuf[:, slot, 0:3 * P], bank[SCB + slot][:, 0:3 * P], DH ** -0.5, mask[:],
                                            ALU.mult, ALU.add))
                V.tensor_reduce(stat[:, ND + 6 * slot:ND + 6 * slot + 1], pbuf[:, slot, 0:P], X, ALU.max, negate=True)
                V.tensor_reduce(stat[:, ND + 6 * slot + 1:ND + 6 * slot + 2], pbuf[:, slot, P:3 * P], X, ALU.max,
                                negate=True).then_inc(s_mx, 1)

            def head_out(h):
                half = slice(64 * (h % 2), 64 * (h % 2) + 64)
                dve.wait_ge(s_pv, h + 1)
                V.tensor_copy(ya[half, h // 2], bank[OUB][half, 0:T]).then_inc(s_pve, 1)

            dve.wait_ge(s_const, 7)
            masked_max(0)
            for h in range(HEADS):
                if h + 1 < HEADS:
                    masked_max(h + 1)
                normalise(h, (P, 2 * P))
                unit(U_CK + h)
                if h:
                    head_out(h - 1)
            head_out(HEADS - 1)
            for c in range(DC):
                src, gain = (a_, "gn_lru") if c < LC else (ya, "gn_attn")
                dve.wait_ge(s_gh, c + 1)
                V.scalar_tensor_tensor(mixt[:, c, 1], src[:, c % LC], pcol(gain, c % LC), mixt[:, c, 0].bitcast(F32),
                                       ALU.mult, ALU.subtract).then_inc(s_gl, 1)
            dve.wait_ge(s_gmm, 1)
            V.tensor_scalar(stat[:, SS + 12:SS + 16], bank[OUB][:, 0:4], 1.0 / 512, EPS, ALU.mult, ALU.add).then_inc(s_var, 1)
            dve.wait_ge(s_std, 3)
            rs = stat[:, RS + 12:RS + 16]
            link(V.reciprocal(rs, rs))
            for u in range(U_OUT, U_CQ):
                unit(u)
                dve.wait_ge(s_wmm, u + 1)
                c0 = WCOL * (u - U_OUT)
                for g in range(2):
                    for t in range(TT):
                        xc = xr[:, t, c0:c0 + WCOL]
                        last = V.scalar_tensor_tensor(xc, acc[:, 2 * (u % 2) + t, WCOL * g:WCOL * g + WCOL],
                                                      rs[:, 2 * g + t:2 * g + t + 1], xc, ALU.mult, ALU.add)
                        if g == 0 and t == 1:
                            link(last)
                last.then_inc(s_wevd, 1)

            variance(2, 3)
            scaled(2, 4, xr, xs)
            t_low(2, "ln_cross", xt)
            for u in range(U_CQ, U_CO):
                unit(u)
            for h in range(CHEADS):
                n = HEADS + h
                slot = n % 2
                st = ND + 6 * slot
                dve.wait_ge(s_sc, n + 1)
                link(V.tensor_reduce(stat[:, st:st + 2], bank[SCB + slot][:].rearrange("p (t k) -> p t k", t=TT), X, ALU.max))
                dve.wait_ge(s_pt, n - 1)
                V.tensor_scalar(stat[:, st:st + 2], stat[:, st:st + 2], -CDH ** -0.5, None, ALU.mult).then_inc(s_mx, 1)
                normalise(n, (T, T))
                dve.wait_ge(s_gh, DC + h + 1)
                V.tensor_tensor(oct_[:, 2 * h:2 * h + 2, 1], bank[OUB][:].rearrange("p (c t) -> p c t", c=2),
                                oct_[:, 2 * h:2 * h + 2, 0].bitcast(F32), ALU.subtract).then_inc(s_cl, 1)
            for u in range(U_CO, U_PQ):
                unit(u)
                dve.wait_ge(s_wmm, u + 1)
                c0 = WCOL * (u - U_CO)
                for t in range(TT):
                    xc = xr[:, t, c0:c0 + WCOL]
                    last = V.tensor_tensor(xc, acc[:, 2 * (u % 2) + t, 0:WCOL], xc, ALU.add)
                last.then_inc(s_wevd, 1)
            variance(3, 4)
            scaled(3, 5, xr, xs)
            t_low(3, "ln_ffn", xt)
            for u in range(U_PQ, NU):
                unit(u)

            def split_low(k, ready, have):
                dve.wait_ge(*have)
                V.tensor_tensor(hl[:, k % 2, 1], raw[:, k // 2, k % 2], hl[:, k % 2, 0].bitcast(F32), ALU.subtract).then_inc(ready, 1)

            ROUTE_LINKS = 20
            chain0 = chain[0]

            def route_pass(it, part):
                n = [5 * part]

                def rlink(ins):
                    n[0] += 1
                    ins.then_inc(s_dve, 1)
                    dve.wait_ge(s_dve, it * ROUTE_LINKS + (chain0 + n[0]))

                def best16(src, work, k):
                    rlink(V.max(topv[:, k, 0:8], src))
                    rlink(V.match_replace(work, topv[:, k, 0:8], src, LOWEST))
                    rlink(V.max(topv[:, k, 8:16], work))
                    V.max_index(topi[:, k, 0:8], topv[:, k, 0:8], src)
                    rlink(V.max_index(topi[:, k, 8:16], topv[:, k, 8:16], work))

                if part < 2:
                    best16(srow[:, ds(it, 1), part].rearrange("p o k -> p (o k)"), rwork[:], part)
                    rlink(V.tensor_copy(topf[:, part], topi[:, part]))
                elif part == 2:
                    rlink(V.tensor_tensor(cand[:].rearrange("p (a b) -> p a b", a=TOPK),
                                          topv[:, 0].unsqueeze(2).broadcast_to([P, TOPK, TOPK]),
                                          topv[:, 1].unsqueeze(1).broadcast_to([P, TOPK, TOPK]), ALU.add))
                    best16(cand[:], candw[:], 2)
                else:
                    V.tensor_scalar(posu[:, 0], topi[:, 2], 4, None, ALU.logical_shift_right)
                    rlink(V.tensor_scalar(posu[:, 1], topi[:, 2], 15, None, ALU.bitwise_and))
                    rlink(V.tensor_copy(flat(posf[:]), flat(posu[:])))
                    rlink(V.tensor_tensor(eq[:].rearrange("p a k b -> p (a k) b"),
                                          flat(posf[:]).unsqueeze(2).broadcast_to([P, 2 * TOPK, TOPK]),
                                          iota[:, 0:TOPK].unsqueeze(1).broadcast_to([P, 2 * TOPK, TOPK]), ALU.is_equal))
                    rlink(V.tensor_tensor(eq[:], eq[:], topf[:].unsqueeze(2).broadcast_to([P, 2, TOPK, TOPK]), ALU.mult))
                    kr = krow[:].rearrange("p a t (h k) -> p a (t h) k", k=TOPK)
                    rlink(V.tensor_reduce(kr[:, 0:2, ds(it, 1)].rearrange("p a o k -> p a (o k)"), eq[:], X, ALU.add))
                    V.tensor_scalar(kr[:, 2, ds(it, 1)], topv[:, 2:3], topv[:, 2, 0:1], None, ALU.subtract).then_inc(s_rt, 1)

            split_low(0, s_ul, (s_uh, 1))
            split_low(1, s_ul, (s_uh, 2))
            dve.wait_ge(s_ke, 8)

            def u_pass(it, last):
                for jj in range(JPB):
                    if not (last and jj + 2 >= JPB):
                        split_low((jj + 2) % 4, s_ul, (s_uh, it * JPB + (jj + 3)))
                    if jj % 2 == 0:
                        route_pass(it, jj // 2)

            for it in range(KEYS // JPB):
                u_pass(it, it == KEYS // JPB - 1)
            chain[0] = chain0 + ROUTE_LINKS * (KEYS // JPB)
            dve.wait_ge(s_ge, 1)
            gk = krow[:, 2].rearrange("p t (h k) -> p (t h) k", k=TOPK)
            gs = stat[:, GS:GS + TT * PH]
            link(V.tensor_reduce(gs, gk, X, ALU.add))
            link(V.reciprocal(gs, gs))
            V.tensor_tensor(gk, gk, gs.unsqueeze(2).broadcast_to([P, TT * PH, TOPK]), ALU.mult).then_inc(s_gr, 1)

            split_low(0, s_vl, (s_vh, 1))
            split_low(1, s_vl, (s_vh, 2))

            dve.wait_ge(s_kte, 1)

            def onehots(t0, slot):
                for k in range(GRP):
                    last = V.tensor_scalar(oh_i[:, slot, k, :], iota[:], kt3[:, 0, ds(t0 + k, 1)], kt3[:, 2, ds(t0 + k, 1)],
                                           ALU.is_equal, ALU.mult)
                last.then_inc(s_oi, 1)

            def weigh(g, t0, slot):
                dve.wait_ge(s_gm, g + 1)
                aw = act_w[:, :, ds(t0, GRP)]
                V.tensor_tensor(aw, bank[slot][:].rearrange("p (t j) -> p j t", t=GRP), aw, ALU.mult).then_inc(s_gw, 1)

            dve.wait_ge(s_ua, KEYS)
            onehots(0, 0)
            onehots(GRP, 1)
            with dve.Fori(0, T // GRP // 2 - 1) as it:
                for slot in range(2):
                    weigh(it * 2 + slot, it * (2 * GRP) + GRP * slot, slot)
                    onehots(it * (2 * GRP) + GRP * (slot + 2), slot)
            for slot in range(2):
                g = T // GRP - 2 + slot
                weigh(g, GRP * g, slot)

            def a_low(j, slot):
                dve.wait_ge(s_Wh, j + 1)
                V.tensor_tensor(whl[:, slot, 1], act_w[:, ds(j, 1)].rearrange("p o t -> p (o t)"), whl[:, slot, 0].bitcast(F32),
                                ALU.subtract).then_inc(s_Wl, 1)

            a_low(0, 0)
            a_low(1, 1)

            def v_pass(it, last):
                for jj in range(4):
                    k = jj + 2
                    if last and k >= 4:
                        continue
                    split_low(k % 4, s_vl, (s_vh, it * 4 + (k + 1)))
                    a_low(it * 4 + k, jj % 2)

            with dve.Fori(0, KEYS // 4 - 1) as it:
                v_pass(it, False)
            v_pass(KEYS // 4 - 1, True)
            dve.wait_ge(s_fs, TT)
            V.tensor_scalar(stat[:, SS:SS + 2], stat[:, SS:SS + 2], 1.0 / D, EPS, ALU.mult, ALU.add).then_inc(s_fv, 1)
            dve.wait_ge(s_fd, 1)
            link(V.reciprocal(stat[:, RS:RS + 2], stat[:, RS:RS + 2]))
            for t in range(TT):
                V.scalar_tensor_tensor(fin[:, t].rearrange("p (a n) -> p a n", a=2), acc[:, 2 * t:2 * t + 2, :],
                                       stat[:, RS + t:RS + t + 1], gfin[:].rearrange("p (a n) -> p a n", a=2),
                                       ALU.mult, ALU.mult).then_inc(s_fin, 1)

        @block.tensor
        def _(pe):
            def transposes(k, src):
                pe.wait_ge(s_xs, k + 1)
                for c in range(DC):
                    for t in range(TT):
                        o = T * (c % 2) + P * t
                        last = pe.transpose(bank[c // 2][:, o:o + P], src[:, t, P * c:P * c + P], ident[:])
                    if c % 2:
                        last.then_inc(s_tr, 1)

            def unit(u, xin):
                pe.wait_ge(s_wl, u + 1)
                if u >= 2:
                    wevac(pe, u - 2)
                kind = UNITS[u][2]
                wh, wl = wsp[:, u % 2, 0], wsp[:, u % 2, 1]
                for k in range(2):
                    groups = ((0, LC), (LC, DC)) if kind == "groups" else ((0, DC),)
                    for g, (c0, c1) in enumerate(groups):
                        dst = acc[:, 2 * (u % 2) + k, WCOL * g:WCOL * g + WCOL]
                        for c in range(c0, c1):
                            if kind == "cols":
                                q = slice(P * k, P * k + P)
                                ops = ((wh[:, c, q], xin[:, c, 0]), (wh[:, c, q], xin[:, c, 1]), (wl[:, c, q], xin[:, c, 0]))
                            else:
                                q = slice(P * k, P * k + P)
                                ops = ((xin[:, c, 0, q], wh[:, c]), (xin[:, c, 0, q], wl[:, c]), (xin[:, c, 1, q], wh[:, c]))
                            for n, (a, b) in enumerate(ops):
                                last = pe.matmul(dst, a, b, start=(c == c0 and n == 0), stop=(c == c1 - 1 and n == 2))
                last.then_inc(s_wmm, 1)

            def scores(h):
                half = slice(64 * (h % 2), 64 * (h % 2) + 64)
                b = bank[SCB + h % 2]
                if h >= 2:
                    pe.wait_ge(s_mx, h - 1)
                pe.matmul(b[:, 0:P], qt[half, h // 2, 0:P], ktt[half, h // 2, 0:P], start=True, stop=True)
                pe.matmul(b[:, P:3 * P], qt[half, h // 2, P:2 * P], ktt[half, h // 2, :], start=True, stop=True).then_inc(s_sc, 1)

            def probs_t(h):
                pe.wait_ge(s_pn, h + 1)
                if h >= 1:
                    pe.wait_ge(s_pe, h)
                p = pbuf[:, h % 2]
                pe.transpose(bank[TRB][:, 0:P], p[:, 0:P], ident[:])
                pe.transpose(bank[TRB][:, P:2 * P], p[:, P:2 * P], ident[:])
                pe.transpose(bank[TRB][:, 2 * P:3 * P], p[:, 2 * P:3 * P], ident[:]).then_inc(s_pt, 1)

            def head_pv(h):
                half = slice(64 * (h % 2), 64 * (h % 2) + 64)
                pe.wait_ge(s_pe, h + 1)
                if h >= 1:
                    pe.wait_ge(s_pve, h)
                vh = slice(DH * h, DH * h + DH)
                pe.matmul(bank[OUB][half, 0:T], v_sb[:, 0, vh], ptr[:, h % 2, 0:T], start=True, stop=False)
                pe.matmul(bank[OUB][half, P:T], v_sb[:, 1, vh], ptr[:, h % 2, T:T + P], start=False, stop=True).then_inc(s_pv, 1)

            pe.wait_ge(s_const, 7)
            transposes(0, xs)
            pe.wait_ge(s_tl, DC)
            unit(0, xt)
            unit(1, xt)
            transposes(1, mr)
            unit(2, xt)
            unit(3, xt)
            pe.wait_ge(s_bd, 64)
            pe.wait_ge(s_cv, CONV * LC)
            pe.wait_ge(s_tl, 2 * DC)
            for mch in range(LC):
                pe.matmul(bank[mch][:, 0:T], bd[:, 0, mch], cv_[:, mch], start=True, stop=True)
                pe.matmul(bank[mch][:, T:2 * T], bd[:, 1, mch], cv_[:, mch], start=True, stop=True).then_inc(s_lg, 1)
            for u in range(4, 10):
                unit(u, xt)
            wevac(pe, U_V + 1)
            pe.wait_ge(s_sg, LC)
            scores(0)
            for h in range(HEADS):
                if h + 1 < HEADS:
                    scores(h + 1)
                unit(U_CK + h, memt)
                probs_t(h)
                if h:
                    head_pv(h - 1)
            head_pv(HEADS - 1)
            pe.wait_ge(s_pve, HEADS)
            pe.wait_ge(s_gss, 2)
            for g, sq in enumerate((r_, i_)):
                for t in range(TT):
                    for c in range(LC):
                        last = pe.matmul(bank[OUB][:, 2 * g + t:2 * g + t + 1], sq[:, c, P * t:P * t + P], ones[:, 0:1],
                                         start=(c == 0), stop=(c == LC - 1))
            last.then_inc(s_gmm, 1)
            pe.wait_ge(s_gl, DC)
            for u in range(U_OUT, U_CQ):
                unit(u, mixt)
            transposes(2, xs)
            pe.wait_ge(s_tl, 3 * DC)
            for u in range(U_CQ, U_CO):
                unit(u, xt)
            wevac(pe, U_CO - 1)

            def cross_scores(h):
                n = HEADS + h
                b = bank[SCB + n % 2]
                pe.wait_ge(s_ex, n - 1)
                for t in range(TT):
                    for c in range(2):
                        last = pe.matmul(b[:, T * t:T * t + T], qct[:, 2 * h + c, P * t:P * t + P], kct[:, 2 * h + c, :],
                                         start=(c == 0), stop=(c == 1))
                last.then_inc(s_sc, 1)

            def cross_probs_t(h):
                n = HEADS + h
                pe.wait_ge(s_pn, n + 1)
                pe.wait_ge(s_pe, n)
                for t in range(TT):
                    for k in range(TT):
                        last = pe.transpose(bank[TRB][:, T * k + P * t:T * k + P * t + P], pbuf[:, n % 2, T * t + P * k:T * t + P * k + P],
                                            ident[:])
                last.then_inc(s_pt, 1)

            def cross_pv(h):
                n = HEADS + h
                pe.wait_ge(s_pe, n + 1)
                if h:
                    pe.wait_ge(s_cl, h)
                for c in range(2):
                    for k in range(TT):
                        d0 = CDH * h + P * c
                        last = pe.matmul(bank[OUB][:, T * c:T * c + T], vc[:, k, d0:d0 + P], ptr[:, n % 2, T * k:T * k + T],
                                         start=(k == 0), stop=(k == TT - 1))
                last.then_inc(s_pv, 1)

            cross_scores(0)
            for h in range(CHEADS):
                if h + 1 < CHEADS:
                    cross_scores(h + 1)
                cross_probs_t(h)
                cross_pv(h)
            pe.wait_ge(s_cl, CHEADS)
            for u in range(U_CO, U_PQ):
                unit(u, oct_)
            transposes(3, xs)
            pe.wait_ge(s_tl, 4 * DC)
            for u in range(U_PQ, NU):
                unit(u, xt)
            pe.wait_ge(s_keys, 16)
            wevac(pe, NU - 1)
            for t in range(TT):
                for b in range(4):
                    n = 4 * t + b
                    if n >= 4:
                        pe.wait_ge(s_ke, n - 3)
                    for k in range(4):
                        hp = 4 * b + k
                        last = pe.matmul(bank[b][:, P * k:P * k + P], qpt[:, hp, P * t:P * t + P], keys[:, hp], start=True, stop=True)
                    last.then_inc(s_ks, 1)

            def u_keys(it, first):
                for k in range(4):
                    pe.wait_ge(s_ul, it * 4 + (k + 1))
                    if first:
                        pe.wait_ge(s_ke, 5 + k)
                    else:
                        pe.wait_ge(s_ua, it * 4 + (k - 3))
                    uh = hl[:, k % 2, 0].rearrange("p (c i) -> p c i", c=DC)
                    ul = hl[:, k % 2, 1].rearrange("p (c i) -> p c i", c=DC)
                    for c in range(DC):
                        pe.matmul(bank[k][:, 0:T], uh[:, c], xt[:, c, 0], start=(c == 0), stop=False)
                        pe.matmul(bank[k][:, 0:T], uh[:, c], xt[:, c, 1], start=False, stop=False)
                        last = pe.matmul(bank[k][:, 0:T], ul[:, c], xt[:, c, 0], start=False, stop=(c == DC - 1))
                    last.then_inc(s_um, 1)

            u_keys(0, True)
            with pe.Fori(1, KEYS // 4) as it:
                u_keys(it, False)

            for t in range(TT):
                for n in range(2):
                    pe.matmul(acc[:, 2 * t + n], ident[:], xr[:, t, 512 * n:512 * n + 512], start=True, stop=False, skip_group_check=True)
            pe.wait_ge(s_gr, 1)
            pe.wait_ge(s_ua, KEYS)
            for k in range(3):
                for t in range(TT):
                    last = pe.transpose(bank[k // 2][:, T * (k % 2) + P * t:T * (k % 2) + P * t + P], krow[:, k, t], ident[:])
            last.then_inc(s_ktr, 1)
            pe.wait_ge(s_kte, 1)

            def route(g, slot, first):
                pe.wait_ge(s_oi, g + 1)
                pe.wait_ge(s_oj, g + 1)
                if not first:
                    pe.wait_ge(s_gw, g - 1)
                for k in range(GRP):
                    last = pe.matmul(bank[slot][:, P * k:P * k + P], oh_i[:, slot, k], oh_j[:, slot, k], start=True, stop=True)
                last.then_inc(s_gm, 1)

            for slot in range(2):
                route(slot, slot, True)
            with pe.Fori(1, T // GRP // 2) as it:
                for slot in range(2):
                    route(it * 2 + slot, slot, False)

            def v_key(j, slot, last_key=False):
                pe.wait_ge(s_vl, j + 1)
                pe.wait_ge(s_Wl, j + 1)
                vh, vl = hl[:, slot, 0], hl[:, slot, 1]
                for t in range(TT):
                    ah, al = whl[:, slot, 0, P * t:P * t + P], whl[:, slot, 1, P * t:P * t + P]
                    for k, (a, b) in enumerate(((ah, vh), (ah, vl), (al, vh))):
                        for n in range(2):
                            last = pe.matmul(acc[:, 2 * t + n], a, b[:, 512 * n:512 * n + 512], start=False,
                                             stop=last_key and k == 2, skip_group_check=True)
                last.then_inc(s_vm, 1)

            with pe.Fori(0, KEYS // 2 - 1) as it:
                for slot in range(2):
                    v_key(it * 2 + slot, slot)
            v_key(KEYS - 2, 0)
            v_key(KEYS - 1, 1, last_key=True)


def kernel(**inputs):
    import numpy as np
    import concourse.bacc as bacc
    from concourse.bass_utils import run_bass_kernel_spmd as run

    def chunks(a, n):
        return np.asarray(a).reshape(-1, n, P).transpose(2, 0, 1).reshape(P, -1)

    i = {k: np.asarray(a) for k, a in inputs.items()}
    par = np.concatenate([
        chunks(i["ln_mix_g"][0], DC), chunks(i["ln_mem_g"][0], DC), chunks(i["ln_cross_g"][0], DC), chunks(i["ln_ffn_g"][0], DC),
        chunks(i["gn_lru_g"][0], LC), chunks(i["gn_attn_g"][0], LC), chunks(i["conv_w"][0], LC), chunks(i["conv_b"][0], LC),
        chunks(i["lru_ba"][0], LC), chunks(i["lru_bx"][0], LC), chunks(i["lru_lambda"][0], LC)], axis=1)
    u_t = i["peer_u"][0].reshape(KEYS, KEYS // 2, 2, DC, P).transpose(1, 4, 2, 3, 0).reshape(KEYS // 2, P, 2, D)
    keys_t = i["peer_subkeys"][0].reshape(2 * PH, KEYS, P).transpose(2, 0, 1)
    arrays = {
        "x": i["x"][0], "mem": i["mem"][0], "par": par, "wa": i["lru_wa"][0], "wx": i["lru_wx"][0],
        "w_in": i["w_in"][0], "w_ck": i["w_ck"][0], "w_cv": i["w_cv"][0], "w_out": i["w_out"][0], "w_cq": i["w_cq"][0],
        "w_co": i["w_co"][0], "w_pq": i["peer_wq"][0], "keys_t": keys_t, "u_t": u_t, "v": i["peer_v"][0],
        "g_final": i["ln_final_g"],
    }
    arrays = {k: np.ascontiguousarray(a) for k, a in arrays.items()}
    nc = bacc.Bacc("TRN2", target_bir_lowering=False, num_devices=1)
    ap = {k: nc.dram_tensor(k, a.shape, mybir.dt.from_np(a.dtype), kind="ExternalInput").ap() for k, a in arrays.items()}
    out = nc.dram_tensor("out", (T, D), F32, kind="ExternalOutput").ap()
    w = {k: ap[k] for k in ("w_in", "w_ck", "w_cv", "w_out", "w_cq", "w_co", "w_pq")}
    build(nc, ap["x"], ap["mem"], ap["par"], ap["wa"], ap["wx"], w, ap["keys_t"], ap["u_t"], ap["v"], ap["g_final"], out)
    r = run(nc, [arrays], core_ids=[0])
    return r.results[0]["out"].reshape(1, T, D)
```

```python
from contextlib import ExitStack

import concourse.bass as bass
from concourse import mybir

F32 = mybir.dt.float32
F32R = mybir.dt.float32r
U32 = mybir.dt.uint32
ALU = mybir.AluOpType
ACT = mybir.ActivationFunctionType
X = mybir.AxisListType.X
ds = bass.ds

P = 128
T, D = 256, 1024
TT, DC = T // P, D // P
LC = 4
HEADS, DH = 8, 64
CHEADS, CDH = 4, 256
PH, TOPK, KEYS = 8, 16, 128
CONV = 4
EPS = 1e-6
NEG = -1e30
LOWEST = -3.0e38
WCOL = 256

PAR = {}
_at = 0
for _name, _n in (("ln_mix", DC), ("ln_mem", DC), ("ln_cross", DC), ("ln_ffn", DC), ("gn_lru", LC), ("gn_attn", LC),
                  ("conv_w", CONV * LC), ("conv_b", LC), ("ba", LC), ("bx", LC), ("lam", LC)):
    PAR[_name] = (_at, _n)
    _at += _n
NPAR = _at

UNITS = ([("w_in", WCOL * i, "cols") for i in range(8)] + [("w_in", WCOL * i, "rows") for i in range(8, 10)]
         + [("w_ck", WCOL * i, "cols") for i in range(4)] + [("w_cv", WCOL * i, "rows") for i in range(4)]
         + [("w_out", WCOL * i, "groups") for i in range(4)]
         + [("w_cq", WCOL * i, "cols") for i in range(4)] + [("w_co", WCOL * i, "rows") for i in range(4)]
         + [("w_pq", WCOL * i, "cols") for i in range(8)])
U_LRU, U_GATE, U_Q, U_K, U_V, U_CK, U_CV, U_OUT, U_CQ, U_CO, U_PQ = 0, 2, 4, 6, 8, 10, 14, 18, 22, 26, 30
NU = len(UNITS)
WRAW = 4
DVE_EVAC = set(range(U_OUT, U_CQ)) | set(range(U_CO, U_PQ))

JPB = 8
GRP = 4


def build(nc, x, mem, par, wa, wx, w, keys_t, u_t, v, g_final, out):
    ctx = ExitStack()
    with ctx:
        base = 16512

        def at(name, off, shape, dt=F32):
            return nc.alloc_sbuf_tensor_at(name, [P] + shape, dt, offset=base + off)

        def sem(name):
            return ctx.enter_context(nc.semaphore(name))

        K = 1024
        act_w = at("act_w", 0, [KEYS, T])
        xr = at("xr", 128 * K, [TT, D])
        xt = at("xt", 136 * K, [DC, 2, T], F32R)
        raw = at("raw", 152 * K, [2, 2, D])
        hl = at("hl", 168 * K, [2, 2, D], F32R)
        hl2 = at("hl2", 128 * K, [2, D], F32R)
        hl3v = at("hl3v", 136 * K, [2, D], F32R)
        gfin = at("gfin", 144 * K, [D])
        sqd = at("sqd", 148 * K, [2, GRP, P])
        fin = at("fin", 128 * K, [TT, D])
        m = 184 * K
        ident = at("ident", m, [P]); m += 512
        iota = at("iota", m, [P]); m += 512
        pars = at("pars", m, [NPAR]); m += 288
        ones = at("ones", m, [8]); m += 32
        stat = at("stat", m, [104]); m += 416
        kt3 = at("kt3", m, [3, T]); m += 3 * K
        krow = at("krow", m, [3, TT, P]); m += 3 * K
        oh_at = m
        hl3u = at("hl3u", m, [2, D], F32R)
        oh_i = at("oh_i", m, [2, GRP, P])
        oh_j0 = at("oh_j0", m + 4 * K, [2, GRP, P])
        whl = at("whl", m, [4, 2, T], F32R)
        m += 8 * K
        oh_j1 = at("oh_j1", m, [2, GRP, P])
        cand = at("cand", m, [256])
        candw = at("candw", m + K, [256])
        rwork = at("rwork", m + 2 * K, [P])
        eq = at("eq", m + 2 * K + 512, [2, TOPK, TOPK])
        topv = at("topv", m + 4 * K + 512, [3, TOPK])
        topi = at("topi", m + 4 * K + 704, [3, TOPK], U32)
        posu = at("posu", m + 4 * K + 896, [2, TOPK], U32)
        posf = at("posf", m + 4 * K + 1024, [2, TOPK])
        topf = at("topf", m + 4 * K + 1152, [2, TOPK])
        m += 5 * K + 256
        mask = at("mask", m, [3 * P]); m += 1536
        assert base + m <= 229344
        wraw = at("wraw", 0, [WRAW, DC, WCOL])
        wsp = at("wsp", 32 * K, [2, 2, DC, WCOL], F32R)
        mr = at("mr", 64 * K, [TT, D])
        v_sb = at("v_sb", 64 * K, [TT, 512])
        ya = at("ya", 68 * K, [LC, T])
        memt = at("memt", 72 * K, [DC, 2, T], F32R)
        qct = at("qct", 72 * K, [DC, T])
        keys = at("keys", 80 * K, [2 * PH, KEYS])
        xs = at("xs", 88 * K, [TT, D])
        pbuf = at("pbuf", 88 * K, [2, 512])
        ptr = at("ptr", 92 * K, [2, 512])
        mixt = at("mixt", 96 * K, [DC, 2, T], F32R)
        oct_ = at("oct", 96 * K, [DC, 2, T], F32R)
        qpt = at("qpt", 96 * K, [2 * PH, T])
        kct = at("kct", 112 * K, [DC, T])
        bd = at("bd", 120 * K, [2, LC, P])
        vc = at("vc", 120 * K, [TT, D])
        srow = at("srow", 112 * K, [TT * PH, 2, KEYS])
        cx = at("cx", oh_at, [LC, T + CONV - 1])
        lru = at("lru", 152 * K, [8, LC, T])
        cv_, r_, i_, a_, th_, gel = (lru[:, k] for k in range(6))
        qt, ktt = lru[:, 6], lru[:, 7]

        def flat(ap):
            return ap.rearrange("p a b -> p (a b)")

        bank = [ctx.enter_context(nc.psum_tensor(f"bank{i}", [P, 512], F32)) for i in range(4, 8)]
        acc = ctx.enter_context(nc.psum_tensor("acc", [P, 4, 512], F32))

        SS, RS = 0, 16
        ND = 32
        SP = 48
        QS = 96
        GS = 72
        s_par, s_x, s_mem, s_bd, s_keys, s_gf, s_out = (sem(n) for n in (
            "s_par", "s_x", "s_mem", "s_bd", "s_keys", "s_gf", "s_out"))
        s_wr = [sem(f"s_wraw{i}") for i in range(WRAW)]
        s_wh, s_wl, s_wmm, s_weva, s_wevd = (sem(n) for n in ("s_w_high", "s_w_low", "s_w_mm", "s_w_evac_act", "s_w_evac_dve"))
        s_const = sem("s_const")
        s_sq, s_var, s_std, s_xs, s_tr, s_th, s_tl = (sem(n) for n in (
            "s_squares", "s_variance", "s_deviation", "s_scaled", "s_transposed", "s_t_high", "s_t_low"))
        s_pool, s_dve, s_act = sem("s_pool_chain"), sem("s_dve_chain"), sem("s_act_chain")
        s_spe, s_spc = sem("s_softplus_exp"), sem("s_softplus_done")
        s_cv, s_lg, s_sg, s_at, s_b2, s_sqr, s_y = (sem(n) for n in (
            "s_conv", "s_lru_gate_mm", "s_lru_sigmoid", "s_lru_a_tanh", "s_lru_1ma2", "s_lru_sqrt", "s_lru_y"))
        s_gss, s_gmm, s_gh, s_gl = (sem(n) for n in ("s_group_squares", "s_group_sums", "s_group_high", "s_group_low"))
        s_sc, s_mx, s_ex, s_pn, s_pt, s_pe, s_pv, s_pve = (sem(n) for n in (
            "s_scores", "s_att_max", "s_att_exp", "s_att_probs", "s_att_transposed", "s_att_probs_t", "s_att_pv", "s_att_out"))
        s_cl = sem("s_cross_low")
        s_ks, s_ke, s_rt, s_ge, s_gr, s_ktr, s_kte = (sem(n) for n in (
            "s_key_scores", "s_key_rows", "s_routed", "s_gate_exp", "s_gates", "s_key_transposed", "s_key_cols"))
        s_raw = [sem(f"s_raw{i}") for i in range(2)]
        s_uh, s_ul, s_um, s_ua = (sem(n) for n in ("s_u_high", "s_u_low", "s_u_mm", "s_u_gelu"))
        s_oi, s_ojp, s_oja, s_sqd, s_gm, s_gw = (sem(n) for n in (
            "s_onehot_i", "s_onehot_j_pool", "s_onehot_j_act", "s_sq_distance", "s_route_mm", "s_route_mul"))
        s_seed = sem("s_seed")
        s_vh, s_vl, s_Wh, s_Wl, s_vm = (sem(n) for n in ("s_v_high", "s_v_low", "s_a_high", "s_a_low", "s_v_mm"))
        s_fs, s_fv, s_fd, s_fin = (sem(n) for n in ("s_fin_squares", "s_fin_var", "s_fin_dev", "s_fin"))

        def pcol(name, c, n=1):
            o = PAR[name][0] + c
            return pars[:, o:o + n]

        def rows(ap):
            return ap.rearrange("(t p) d -> p t d", p=P)

        wd = {n: a.rearrange("(c p) n -> p c n", p=P) for n, a in w.items()}
        vd = v.rearrange("(i q j) d -> q i j d", i=KEYS, j=2)
        SCB, TRB, OUB = 0, 2, 3

        def wevac(eng, u):
            if u in DVE_EVAC:
                eng.wait_ge(s_wevd, sum(1 for k in DVE_EVAC if k <= u))
            else:
                eng.wait_ge(s_weva, sum(1 for k in range(u + 1) if k not in DVE_EVAC))

        def eslot(k, part, second):
            return (hl[:, 0], hl[:, 1], hl2, hl3v if second else hl3u)[k][:, part]

        def oh_j(slot):
            return (oh_j0, oh_j1)[slot // 2][:, slot % 2]

        block = ctx.enter_context(nc.Block())

        @block.sync
        def _(sp):
            sp.dma_start(xr[:], rows(x)).then_inc(s_x, 16)
            sp.dma_start(pars[:], par).then_inc(s_par, 16)

            def unit(u):
                name, c0, _ = UNITS[u]
                if u >= WRAW:
                    sp.wait_ge(s_wl, u - WRAW + 1)
                sp.dma_start(wraw[:, u % WRAW], wd[name][:, :, c0:c0 + WCOL]).then_inc(s_wr[u % WRAW], 16)

            unit(0)
            unit(1)
            sp.dma_start(mr[:], rows(mem)).then_inc(s_mem, 16)
            for u in range(2, WRAW):
                unit(u)
            sp.wait_ge(s_const, 7)
            for k, src in enumerate((wa, wx)):
                for half in range(2):
                    q = slice(64 * half, 64 * half + 64)
                    sp.dma_start(bd[q, k, :, q], src[half::2].rearrange("m d e -> d m e")).then_inc(s_bd, 16)
            for u in range(WRAW, NU):
                unit(u)
                if u == U_PQ + 4:
                    sp.dma_start(keys[:], keys_t).then_inc(s_keys, 16)

            sp.wait_ge(s_pv, 8 + 4)
            for q in range(2):
                sp.dma_start(raw[:, q], u_t[q]).then_inc(s_raw[q], 16)
            with sp.Fori(1, KEYS // 4) as it:
                for q in range(2):
                    sp.wait_ge(s_ul, it * 4 - 4 + 2 * q + 2)
                    sp.dma_start(raw[:, q], u_t[ds(it * 2 + q, 1)].rearrange("o p j d -> (o p) j d")).then_inc(s_raw[q], 16)
            for q in range(2):
                sp.wait_ge(s_ul, KEYS - 4 + 2 * q + 2)
                sp.dma_start(raw[:, q], vd[q]).then_inc(s_raw[q], 16)
            sp.wait_ge(s_um, KEYS)
            sp.dma_start(gfin[:], g_final.rearrange("(o d) -> o d", o=1).broadcast_to([P, D])).then_inc(s_gf, 16)
            with sp.Fori(1, KEYS // 4) as it:
                for q in range(2):
                    sp.wait_ge(s_vl, it * 4 - 4 + 2 * q + 2)
                    sp.dma_start(raw[:, q], vd[ds(it * 2 + q, 1)].rearrange("o i j d -> (o i) j d")).then_inc(s_raw[q], 16)
            for t in range(TT):
                sp.wait_ge(s_fin, t + 1)
                sp.dma_start(out[P * t:P * t + P, :], fin[:, t]).then_inc(s_out, 16)
            sp.wait_ge(s_out, 16 * TT)

        @block.gpsimd
        def _(pool):
            nc.gpsimd.memset(bd[:].rearrange("p a b c -> p (a b c)"), 0.0).then_inc(s_const, 1)
            nc.gpsimd.memset(ident[:], 0.0).then_inc(s_pool, 1)
            nc.gpsimd.memset(mask[:], 0.0).then_inc(s_pool, 1)
            pool.wait_ge(s_pool, 2)
            nc.gpsimd.affine_select(out=ident[:], in_=ident[:], compare_op=ALU.not_equal, fill=1.0, base=0,
                                    pattern=[[-1, P]], channel_multiplier=1).then_inc(s_const, 1)
            nc.gpsimd.affine_select(out=mask[:, 0:P], in_=mask[:, 0:P], compare_op=ALU.is_ge, fill=NEG, base=0,
                                    pattern=[[-1, P]], channel_multiplier=1).then_inc(s_const, 1)
            nc.gpsimd.affine_select(out=mask[:, P:3 * P], in_=mask[:, P:3 * P], compare_op=ALU.is_ge, fill=NEG, base=P,
                                    pattern=[[-1, 2 * P]], channel_multiplier=1).then_inc(s_const, 1)
            nc.gpsimd.iota(iota[:], pattern=[[1, P]], base=0, channel_multiplier=0,
                           allow_small_or_imprecise_dtypes=True).then_inc(s_const, 1)
            nc.gpsimd.memset(ones[:], 1.0).then_inc(s_const, 1)
            nc.gpsimd.memset(cx[:, :, 0:CONV - 1], 0.0).then_inc(s_const, 1)
            pool.wait_ge(s_const, 7)
            pool.wait_ge(s_kte, 3)
            pool.wait_ge(s_um, KEYS)

            for g in range(0, T // GRP, 2):
                if g >= 4:
                    pool.wait_ge(s_gm, g - 3)
                for k in range(GRP):
                    t = GRP * g + k
                    last = nc.gpsimd.tensor_scalar(oh_j(g % 4)[:, k, :], iota[:], kt3[:, 1, t:t + 1], None, ALU.is_equal)
                last.then_inc(s_ojp, 1)

        @block.scalar
        def _(act):
            chain = [0]

            def link(ins):
                chain[0] += 1
                ins.then_inc(s_act, 1)
                act.wait_ge(s_act, chain[0])

            def w_high(u):
                act.wait_ge(s_wr[u % WRAW], 16 * (u // WRAW + 1))
                if u >= 2:
                    act.wait_ge(s_wmm, u - 1)
                nc.scalar.activation(wsp[:, u % 2, 0], wraw[:, u % WRAW], ACT.Copy).then_inc(s_wh, 1)

            def unit(u):
                if u + 2 < NU:
                    w_high(u + 2)
                if u in DVE_EVAC:
                    return
                act.wait_ge(s_wmm, u + 1)
                dst = unit_dst(u)
                for k in range(2):
                    last = nc.scalar.activation(dst(k), acc[:, 2 * (u % 2) + k, 0:WCOL], ACT.Copy)
                last.then_inc(s_weva, 1)

            def squares(n, src, junk):
                for t in range(TT):
                    last = nc.scalar.activation(junk[:, t], src[:, t], ACT.Square, accum_out=stat[:, SS + 2 * n + t:SS + 2 * n + t + 1])
                last.then_inc(s_sq, 1)

            def deviation(n, k):
                act.wait_ge(s_var, k)
                nc.scalar.activation(stat[:, RS + 2 * n:RS + 2 * n + 2], stat[:, SS + 2 * n:SS + 2 * n + 2], ACT.Sqrt).then_inc(s_std, 1)

            def t_high(k, gain, dst):
                for c in range(DC):
                    if c % 2 == 0:
                        act.wait_ge(s_tr, 4 * k + c // 2 + 1)
                    nc.scalar.activation(dst[:, c, 0], bank[c // 2][:, T * (c % 2):T * (c % 2) + T], ACT.Copy,
                                         scale=pcol(gain, c)).then_inc(s_th, 1)

            def unit_dst(u):
                def cols(dst, u0):
                    return lambda k: dst[:, 2 * (u - u0) + k]

                def token_rows(dst, u0):
                    return lambda k: dst[:, k, WCOL * (u - u0):WCOL * (u - u0) + WCOL]

                if u < U_GATE:
                    return lambda k: cx[:, 2 * u + k, CONV - 1:]
                for u1, f, dst, u0 in ((U_Q, cols, gel, U_GATE), (U_K, cols, qt, U_Q), (U_V, cols, ktt, U_K),
                                       (U_CK, token_rows, v_sb, U_V), (U_CV, cols, kct, U_CK), (U_OUT, token_rows, vc, U_CV),
                                       (U_CO, cols, qct, U_CQ), (NU, cols, qpt, U_PQ)):
                    if u < u1:
                        return f(dst, u0)

            act.wait_ge(s_x, 16)
            squares(0, xr, xs)
            deviation(0, 1)
            w_high(0)
            act.wait_ge(s_par, 16)
            t_high(0, "ln_mix", xt)
            w_high(1)
            act.wait_ge(s_mem, 16)
            squares(1, mr, kct[:].rearrange("p (t c) n -> p t (c n)", t=TT))
            deviation(1, 2)
            act.wait_ge(s_const, 7)
            for u in (0, 1):
                unit(u)
            t_high(1, "ln_mem", memt)
            act.wait_ge(s_spe, 1)
            nc.scalar.activation(stat[:, SP + 4:SP + 8], stat[:, SP:SP + 4], ACT.Exp, scale=-1.0).then_inc(s_spc, 1)
            for u in (2, 3):
                unit(u)
            for mch in range(LC):
                act.wait_ge(s_lg, mch + 1)
                nc.scalar.activation(r_[:, mch], bank[mch][:, 0:T], ACT.Sigmoid, bias=pcol("ba", mch))
                nc.scalar.activation(i_[:, mch], bank[mch][:, T:2 * T], ACT.Sigmoid, bias=pcol("bx", mch)).then_inc(s_sg, 1)
            for u in (4, 5):
                unit(u)
            act.wait_ge(s_spc, 2)
            act.wait_ge(s_sg, LC)
            for mch in range(LC):
                nc.scalar.activation(a_[:, mch], r_[:, mch], ACT.Exp, scale=stat[:, SP + 20 + mch:SP + 21 + mch])
                last = nc.scalar.activation(th_[:, mch], r_[:, mch], ACT.Tanh, scale=stat[:, SP + 20 + mch:SP + 21 + mch])
            last.then_inc(s_at, 1)
            for u in (6, 7):
                unit(u)
            act.wait_ge(s_weva, 4)
            nc.scalar.activation(gel[:], gel[:], ACT.Gelu).then_inc(s_at, 1)
            act.wait_ge(s_b2, 1)
            nc.scalar.activation(th_[:], th_[:], ACT.Sqrt, scale=-1.0).then_inc(s_sqr, 1)
            unit(8)

            def group_high(c):
                src, gain = (a_, "gn_lru") if c < LC else (ya, "gn_attn")
                nc.scalar.activation(mixt[:, c, 0], src[:, c % LC], ACT.Copy, scale=pcol(gain, c % LC)).then_inc(s_gh, 1)

            def softmax_exp(n, scale, widths, src):
                slot = n % 2
                st = ND + 6 * slot
                act.wait_ge(s_mx, n + 1)
                o = 0
                for t, wdt in enumerate(widths):
                    last = nc.scalar.activation(pbuf[:, slot, o:o + wdt], src[:, o:o + wdt], ACT.Exp, scale=scale,
                                                bias=stat[:, st + t:st + t + 1], accum_out=stat[:, st + 2 + t:st + 3 + t])
                    o += wdt
                last.then_inc(s_ex, 1)

            def probs_t(n, cols):
                slot = n % 2
                act.wait_ge(s_pt, n + 1)
                if n >= 2:
                    act.wait_ge(s_pv, n - 1)
                nc.scalar.activation(ptr[:, slot, 0:cols], bank[TRB][:, 0:cols], ACT.Copy).then_inc(s_pe, 1)

            for h in range(HEADS):
                softmax_exp(h, 1.0, (P, 2 * P), pbuf[:, h % 2])
                unit(9 + h)
                probs_t(h, 3 * P)
                if h == 2:
                    act.wait_ge(s_y, 1)
                    nc.scalar.activation(r_[:], a_[:], ACT.Square).then_inc(s_gss, 1)
                    for c in range(LC):
                        group_high(c)
            for c in range(LC, DC):
                if c == DC - 1:
                    unit(U_OUT - 1)
                act.wait_ge(s_pve, 2 * (c - LC) + 2)
                nc.scalar.activation(i_[:, c - LC], ya[:, c - LC], ACT.Square).then_inc(s_gss, 1)
                group_high(c)
            act.wait_ge(s_var, 3)
            nc.scalar.activation(stat[:, RS + 12:RS + 16], stat[:, SS + 12:SS + 16], ACT.Sqrt).then_inc(s_std, 1)

            def residual_units(u0, n):
                for q in range(4):
                    u = u0 + q
                    if q < 3:
                        unit(u)
                    act.wait_ge(s_wevd, 4 * n + q + 1)
                    for t in range(TT):
                        c = QS + 4 * t + q
                        last = nc.scalar.activation(xs[:, t, WCOL * q:WCOL * q + WCOL], xr[:, t, WCOL * q:WCOL * q + WCOL],
                                                    ACT.Square, accum_out=stat[:, c:c + 1])
                    last.then_inc(s_sq, 1)
                unit(u)

            residual_units(U_OUT, 0)
            deviation(2, 4)
            t_high(2, "ln_cross", xt)

            def cross_exp(h):
                n = HEADS + h
                softmax_exp(n, CDH ** -0.5, (T, T), bank[SCB + n % 2])

            def cross_out(h):
                act.wait_ge(s_pv, HEADS + h + 1)
                nc.scalar.activation(oct_[:, 2 * h:2 * h + 2, 0], bank[OUB][:].rearrange("p (c t) -> p c t", c=2),
                                     ACT.Copy).then_inc(s_gh, 1)

            unit(U_CQ)
            unit(U_CQ + 1)
            cross_exp(0)
            unit(U_CQ + 2)
            probs_t(HEADS, 2 * T)
            cross_exp(1)
            unit(U_CQ + 3)
            cross_out(0)
            probs_t(HEADS + 1, 2 * T)
            cross_exp(2)
            cross_out(1)
            cross_exp(3)
            probs_t(HEADS + 2, 2 * T)
            cross_out(2)
            probs_t(HEADS + 3, 2 * T)
            cross_out(3)
            residual_units(U_CO, 1)
            deviation(3, 5)
            t_high(3, "ln_ffn", xt)
            for u in range(U_PQ, NU):
                unit(u)
            sr = srow[:].rearrange("p (t h) a k -> p t (h a k)", t=TT)
            for n in range(8):
                act.wait_ge(s_ks, n + 1)
                nc.scalar.activation(sr[:, n // 4, 512 * (n % 4):512 * (n % 4) + 512], bank[n % 4][:], ACT.Copy).then_inc(s_ke, 1)

            def split_high(k, landed, free, ready, second=False):
                if landed is not None:
                    act.wait_ge(s_raw[k // 2], landed)
                if free is not None:
                    act.wait_ge(*free)
                nc.scalar.activation(eslot(k, 0, second), raw[:, k // 2, k % 2], ACT.Copy).then_inc(ready, 1)

            def gelu(j, k):
                act.wait_ge(s_um, j + 1)
                nc.scalar.activation(act_w[:, ds(j, 1)].rearrange("p o t -> p (o t)"), bank[k % 4][:, 0:T], ACT.Gelu).then_inc(s_ua, 1)

            act.wait_ge(s_pv, HEADS + CHEADS)
            for k in range(4):
                split_high(k, 16 if k % 2 == 0 else None, (s_seed, 1) if k == 2 else None, s_uh)
            base16 = 16 * (KEYS // 4)

            with act.Fori(0, KEYS // JPB - 1) as it:
                for jj in range(JPB):
                    j = it * JPB + jj
                    split_high(jj % 4, (it * 2 + (jj // 4 + 2)) * 16 if jj % 2 == 0 else None, (s_um, j + 1), s_uh)
                    if jj == JPB - 1:
                        act.wait_ge(s_rt, it + 1)
                    gelu(j, jj)
            act.wait_ge(s_rt, TT * PH)
            nc.scalar.activation(krow[:, 2], krow[:, 2], ACT.Exp).then_inc(s_ge, 1)
            for jj in range(JPB):
                j = KEYS - JPB + jj
                if jj < 4:
                    split_high(jj, base16 if jj % 2 == 0 else None, (s_um, j + 1), s_uh)
                elif jj < 7:
                    split_high(jj - 4, base16 + 16 if jj % 2 == 0 else None, (s_um, j + 1), s_vh, second=True)
                gelu(j, jj)
                if 4 <= jj < 7:
                    nc.scalar.activation(kt3[:, jj - 4], bank[jj - 4][:, T:2 * T], ACT.Copy).then_inc(s_kte, 1)
            split_high(3, None, None, s_vh, second=True)

            act.wait_ge(s_kte, 3)

            def onehots(n, g, t0, slot, first):
                if not first:
                    act.wait_ge(s_gm, g - 3)
                for k in range(GRP):
                    last = nc.scalar.activation(sqd[:, slot // 2, k], iota[:], ACT.Square, scale=-1.0, bias=kt3[:, 1, ds(t0 + k, 1)])
                last.then_inc(s_sqd, 1)
                act.wait_ge(s_sqd, n + 1)
                nc.scalar.activation(oh_j(slot), sqd[:, slot // 2], ACT.Relu, scale=-1.0, bias=ones[:, 0:1]).then_inc(s_oja, 1)

            for slot in (1, 3):
                onehots(slot // 2, slot, GRP * slot, slot, True)
            with act.Fori(1, T // GRP // 4) as it:
                for slot in (1, 3):
                    onehots(it * 2 + slot // 2, it * 4 + slot, it * (4 * GRP) + GRP * slot, slot, False)

            def a_high(j, slot):
                nc.scalar.activation(whl[:, slot, 0], act_w[:, ds(j, 1)].rearrange("p o t -> p (o t)"), ACT.Copy).then_inc(s_Wh, 1)

            act.wait_ge(s_gw, T // GRP)
            for k in range(4):
                a_high(k, k)
            with act.Fori(0, KEYS // 4 - 1) as it:
                for k in range(4):
                    split_high(k, (it + 2) * 16 + base16 if k % 2 == 0 else None, (s_vm, it * 4 + (k + 1)), s_vh, second=True)
                    a_high(it * 4 + (k + 4), k)
            act.wait_ge(s_vm, KEYS)
            act.wait_ge(s_gf, 16)
            for t in range(TT):
                nc.scalar.activation(fin[:, t].rearrange("p (a n) -> p a n", a=2), acc[:, 2 * t:2 * t + 2, :], ACT.Square,
                                     accum_out=stat[:, SS + t:SS + t + 1]).then_inc(s_fs, 1)
            act.wait_ge(s_fv, 1)
            nc.scalar.activation(stat[:, RS:RS + 2], stat[:, SS:SS + 2], ACT.Sqrt).then_inc(s_fd, 1)

        @block.vector
        def _(dve):
            V = nc.vector
            chain = [0]

            def link(ins):
                chain[0] += 1
                ins.then_inc(s_dve, 1)
                dve.wait_ge(s_dve, chain[0])

            def w_low(u):
                dve.wait_ge(s_wh, u + 1)
                V.tensor_tensor(wsp[:, u % 2, 1], wraw[:, u % WRAW], wsp[:, u % 2, 0].bitcast(F32), ALU.subtract).then_inc(s_wl, 1)

            def unit(u):
                if u + 2 < NU:
                    w_low(u + 2)

            def variance(n, k, cols=2, width=D):
                dve.wait_ge(s_sq, k)
                V.tensor_scalar(stat[:, SS + 2 * n:SS + 2 * n + cols], stat[:, SS + 2 * n:SS + 2 * n + cols],
                                1.0 / width, EPS, ALU.mult, ALU.add).then_inc(s_var, 1)

            def scaled(n, k, src, dst):
                dve.wait_ge(s_std, k)
                rs = stat[:, RS + 2 * n:RS + 2 * n + 2]
                link(V.reciprocal(rs, rs))
                for t in range(TT):
                    last = V.tensor_scalar(dst[:, t], src[:, t], rs[:, t:t + 1], None, ALU.mult)
                last.then_inc(s_xs, 1)

            def t_low(k, gain, dst):
                for c in range(DC):
                    dve.wait_ge(s_th, DC * k + c + 2 - c % 2)
                    V.scalar_tensor_tensor(dst[:, c, 1], bank[c // 2][:, T * (c % 2):T * (c % 2) + T], pcol(gain, c),
                                           dst[:, c, 0].bitcast(F32), ALU.mult, ALU.subtract).then_inc(s_tl, 1)

            dve.wait_ge(s_par, 16)
            lam = pcol("lam", 0, LC)
            c4 = lambda k: stat[:, SP + 4 * k:SP + 4 * k + 4]
            V.scalar_tensor_tensor(c4(0), lam, -1.0, lam, ALU.mult, ALU.max).then_inc(s_spe, 1)
            variance(0, 1)
            scaled(0, 1, xr, xs)
            w_low(0)
            t_low(0, "ln_mix", xt)
            w_low(1)
            variance(1, 2)
            scaled(1, 2, mr, mr)
            unit(0)
            unit(1)
            dve.wait_ge(s_weva, 2)
            for s in range(CONV):
                for mch in range(LC):
                    wcol = pcol("conv_w", LC * s + mch)
                    if s:
                        V.scalar_tensor_tensor(cv_[:, mch], cx[:, mch, s:s + T], wcol, cv_[:, mch], ALU.mult, ALU.add).then_inc(s_cv, 1)
                    else:
                        V.tensor_scalar(cv_[:, mch], cx[:, mch, 0:T], wcol, pcol("conv_b", mch), ALU.mult, ALU.add).then_inc(s_cv, 1)
                dve.wait_ge(s_cv, LC * (s + 1))
            t_low(1, "ln_mem", memt)
            unit(2)
            unit(3)
            dve.wait_ge(s_spc, 1)
            e, z, z2, q, sp8 = c4(1), c4(2), c4(3), c4(4), c4(5)
            link(V.tensor_scalar(z, e, 2.0, None, ALU.add))
            link(V.reciprocal(z, z))
            link(V.tensor_tensor(z, z, e, ALU.mult))
            link(V.tensor_tensor(z2, z, z, ALU.mult))
            link(V.tensor_scalar(q, z2, 1.0 / 17, None, ALU.mult))
            for n in (15, 13, 11, 9, 7, 5, 3):
                link(V.scalar_tensor_tensor(q, q, 1.0 / n, z2, ALU.add, ALU.mult))
            link(V.scalar_tensor_tensor(q, q, 1.0, z, ALU.add, ALU.mult))
            link(V.tensor_scalar(z, lam, -1.0, 0.0, ALU.mult, ALU.max))
            link(V.scalar_tensor_tensor(sp8, q, 2.0, z, ALU.mult, ALU.add))
            V.tensor_scalar(sp8, sp8, -8.0, None, ALU.mult).then_inc(s_spc, 1)
            unit(4)
            unit(5)
            dve.wait_ge(s_sg, LC)
            link(V.tensor_tensor(i_[:], i_[:], cv_[:], ALU.mult))
            dve.wait_ge(s_at, 1)
            link(V.tensor_tensor(r_[:], a_[:], a_[:], ALU.mult))
            V.scalar_tensor_tensor(th_[:], r_[:], 1.0, th_[:], ALU.add, ALU.mult).then_inc(s_b2, 1)
            unit(6)
            unit(7)
            dve.wait_ge(s_sqr, 1)
            link(V.tensor_tensor(i_[:], i_[:], th_[:], ALU.mult))
            for mch in range(LC):
                last = V.tensor_tensor_scan(r_[:, mch], a_[:, mch], i_[:, mch], 0.0, ALU.mult, ALU.add)
            link(last)
            unit(8)
            dve.wait_ge(s_at, 2)
            V.tensor_tensor(a_[:], r_[:], gel[:], ALU.mult).then_inc(s_y, 1)

            def normalise(n, widths):
                slot = n % 2
                st = ND + 6 * slot
                dve.wait_ge(s_ex, n + 1)
                link(V.reciprocal(stat[:, st + 4:st + 6], stat[:, st + 2:st + 4]))
                o = 0
                for t, wdt in enumerate(widths):
                    last = V.tensor_scalar(pbuf[:, slot, o:o + wdt], pbuf[:, slot, o:o + wdt], stat[:, st + 4 + t:st + 5 + t],
                                           None, ALU.mult)
                    o += wdt
                last.then_inc(s_pn, 1)

            def masked_max(h):
                slot = h % 2
                dve.wait_ge(s_sc, h + 1)
                if h >= 2:
                    dve.wait_ge(s_pt, h - 1)
                link(V.scalar_tensor_tensor(pbuf[:, slot, 0:3 * P], bank[SCB + slot][:, 0:3 * P], DH ** -0.5, mask[:],
                                            ALU.mult, ALU.add))
                V.tensor_reduce(stat[:, ND + 6 * slot:ND + 6 * slot + 1], pbuf[:, slot, 0:P], X, ALU.max, negate=True)
                V.tensor_reduce(stat[:, ND + 6 * slot + 1:ND + 6 * slot + 2], pbuf[:, slot, P:3 * P], X, ALU.max,
                                negate=True).then_inc(s_mx, 1)

            def head_out(h):
                half = slice(64 * (h % 2), 64 * (h % 2) + 64)
                dve.wait_ge(s_pv, h + 1)
                V.tensor_copy(ya[half, h // 2], bank[OUB][half, 0:T]).then_inc(s_pve, 1)

            dve.wait_ge(s_const, 7)
            masked_max(0)
            def group_low(c):
                src, gain = (a_, "gn_lru") if c < LC else (ya, "gn_attn")
                dve.wait_ge(s_gh, c + 1)
                V.scalar_tensor_tensor(mixt[:, c, 1], src[:, c % LC], pcol(gain, c % LC), mixt[:, c, 0].bitcast(F32),
                                       ALU.mult, ALU.subtract).then_inc(s_gl, 1)

            for h in range(HEADS):
                if h + 1 < HEADS:
                    masked_max(h + 1)
                normalise(h, (P, 2 * P))
                unit(9 + h)
                if h:
                    head_out(h - 1)
                if 3 <= h < 7:
                    group_low(h - 3)
            for c in range(LC, DC - 1):
                group_low(c)
            unit(U_OUT - 1)
            head_out(HEADS - 1)
            group_low(DC - 1)
            dve.wait_ge(s_gmm, 1)
            V.tensor_scalar(stat[:, SS + 12:SS + 16], bank[OUB][:, 0:4], 1.0 / 512, EPS, ALU.mult, ALU.add).then_inc(s_var, 1)
            dve.wait_ge(s_std, 3)
            rs = stat[:, RS + 12:RS + 16]
            link(V.reciprocal(rs, rs))

            def quarter_variance(n, k):
                dve.wait_ge(s_sq, k)
                ss = stat[:, SS + 2 * n:SS + 2 * n + 2]
                link(V.tensor_reduce(ss, stat[:, QS:QS + 8].rearrange("p (t q) -> p t q", t=TT), X, ALU.add))
                V.tensor_scalar(ss, ss, 1.0 / D, EPS, ALU.mult, ALU.add).then_inc(s_var, 1)

            for u in range(U_OUT, U_CQ):
                dve.wait_ge(s_wmm, u + 1)
                c0 = WCOL * (u - U_OUT)
                for g in range(2):
                    for t in range(TT):
                        xc = xr[:, t, c0:c0 + WCOL]
                        last = V.scalar_tensor_tensor(xc, acc[:, 2 * (u % 2) + t, WCOL * g:WCOL * g + WCOL],
                                                      rs[:, 2 * g + t:2 * g + t + 1], xc, ALU.mult, ALU.add)
                        if g == 0 and t == 1:
                            link(last)
                last.then_inc(s_wevd, 1)
                if u < U_CQ - 1:
                    unit(u)
            quarter_variance(2, 2 + 4)
            scaled(2, 4, xr, xs)
            unit(U_CQ - 1)
            t_low(2, "ln_cross", xt)

            def cross_max(h):
                n = HEADS + h
                st = ND + 6 * (n % 2)
                dve.wait_ge(s_sc, n + 1)
                link(V.tensor_reduce(stat[:, st:st + 2], bank[SCB + n % 2][:].rearrange("p (t k) -> p t k", t=TT), X, ALU.max))
                dve.wait_ge(s_pt, n - 1)
                V.tensor_scalar(stat[:, st:st + 2], stat[:, st:st + 2], -CDH ** -0.5, None, ALU.mult).then_inc(s_mx, 1)
                normalise(n, (T, T))

            def cross_low(h):
                dve.wait_ge(s_gh, DC + h + 1)
                V.tensor_tensor(oct_[:, 2 * h:2 * h + 2, 1], bank[OUB][:].rearrange("p (c t) -> p c t", c=2),
                                oct_[:, 2 * h:2 * h + 2, 0].bitcast(F32), ALU.subtract).then_inc(s_cl, 1)

            unit(U_CQ)
            unit(U_CQ + 1)
            cross_max(0)
            unit(U_CQ + 2)
            cross_max(1)
            unit(U_CQ + 3)
            cross_low(0)
            cross_max(2)
            cross_low(1)
            cross_max(3)
            cross_low(2)
            cross_low(3)
            for u in range(U_CO, U_PQ):
                dve.wait_ge(s_wmm, u + 1)
                c0 = WCOL * (u - U_CO)
                for t in range(TT):
                    xc = xr[:, t, c0:c0 + WCOL]
                    last = V.tensor_tensor(xc, acc[:, 2 * (u % 2) + t, 0:WCOL], xc, ALU.add)
                last.then_inc(s_wevd, 1)
                if u < U_PQ - 1:
                    unit(u)
            quarter_variance(3, 2 + 8)
            scaled(3, 5, xr, xs)
            unit(U_PQ - 1)
            t_low(3, "ln_ffn", xt)
            for u in range(U_PQ, NU):
                unit(u)

            def split_low(k, ready, have, second=False):
                dve.wait_ge(*have)
                V.tensor_tensor(eslot(k, 1, second), raw[:, k // 2, k % 2], eslot(k, 0, second).bitcast(F32),
                                ALU.subtract).then_inc(ready, 1)

            ROUTE_LINKS = 20
            chain0 = chain[0]

            def route_pass(it, part):
                n = [5 * part]

                def rlink(ins):
                    n[0] += 1
                    ins.then_inc(s_dve, 1)
                    dve.wait_ge(s_dve, it * ROUTE_LINKS + (chain0 + n[0]))

                def best16(src, work, k):
                    rlink(V.max(topv[:, k, 0:8], src))
                    rlink(V.match_replace(work, topv[:, k, 0:8], src, LOWEST))
                    rlink(V.max(topv[:, k, 8:16], work))
                    V.max_index(topi[:, k, 0:8], topv[:, k, 0:8], src)
                    rlink(V.max_index(topi[:, k, 8:16], topv[:, k, 8:16], work))

                if part < 2:
                    best16(srow[:, ds(it, 1), part].rearrange("p o k -> p (o k)"), rwork[:], part)
                    rlink(V.tensor_copy(topf[:, part], topi[:, part]))
                elif part == 2:
                    rlink(V.tensor_tensor(cand[:].rearrange("p (a b) -> p a b", a=TOPK),
                                          topv[:, 0].unsqueeze(2).broadcast_to([P, TOPK, TOPK]),
                                          topv[:, 1].unsqueeze(1).broadcast_to([P, TOPK, TOPK]), ALU.add))
                    best16(cand[:], candw[:], 2)
                else:
                    V.tensor_scalar(posu[:, 0], topi[:, 2], 4, None, ALU.logical_shift_right)
                    rlink(V.tensor_scalar(posu[:, 1], topi[:, 2], 15, None, ALU.bitwise_and))
                    rlink(V.tensor_copy(flat(posf[:]), flat(posu[:])))
                    rlink(V.tensor_tensor(eq[:].rearrange("p a k b -> p (a k) b"),
                                          flat(posf[:]).unsqueeze(2).broadcast_to([P, 2 * TOPK, TOPK]),
                                          iota[:, 0:TOPK].unsqueeze(1).broadcast_to([P, 2 * TOPK, TOPK]), ALU.is_equal))
                    rlink(V.tensor_tensor(eq[:], eq[:], topf[:].unsqueeze(2).broadcast_to([P, 2, TOPK, TOPK]), ALU.mult))
                    kr = krow[:].rearrange("p a t (h k) -> p a (t h) k", k=TOPK)
                    rlink(V.tensor_reduce(kr[:, 0:2, ds(it, 1)].rearrange("p a o k -> p a (o k)"), eq[:], X, ALU.add))
                    V.tensor_scalar(kr[:, 2, ds(it, 1)], topv[:, 2:3], topv[:, 2, 0:1], None, ALU.subtract).then_inc(s_rt, 1)

            for k in range(4):
                split_low(k, s_ul, (s_uh, k + 1))
            dve.wait_ge(s_ke, 8)
            parts = 0
            for j in range(KEYS - 1):
                if j < KEYS - 4:
                    split_low(j % 4, s_ul, (s_uh, j + 5))
                else:
                    split_low(j % 4, s_vl, (s_vh, j + 5 - KEYS), second=True)
                if parts < 4 * TT * PH and 5 * (j + 1) // 8 > parts:
                    route_pass(parts // 4, parts % 4)
                    parts += 1
                if j == KEYS - JPB:
                    dve.wait_ge(s_ge, 1)
                    gk = krow[:, 2].rearrange("p t (h k) -> p (t h) k", k=TOPK)
                    gs = stat[:, GS:GS + TT * PH]
                    chain[0] = chain0 + ROUTE_LINKS * TT * PH
                    link(V.tensor_reduce(gs, gk, X, ALU.add))
                    link(V.reciprocal(gs, gs))
                    V.tensor_tensor(gk, gk, gs.unsqueeze(2).broadcast_to([P, TT * PH, TOPK]), ALU.mult).then_inc(s_gr, 1)

            dve.wait_ge(s_kte, 3)
            dve.wait_ge(s_ua, KEYS)

            def onehots(t0, slot):
                for k in range(GRP):
                    last = V.tensor_scalar(oh_i[:, slot % 2, k, :], iota[:], kt3[:, 0, ds(t0 + k, 1)], kt3[:, 2, ds(t0 + k, 1)],
                                           ALU.is_equal, ALU.mult)
                last.then_inc(s_oi, 1)

            def weigh(g, t0, slot):
                dve.wait_ge(s_gm, g + 1)
                aw = act_w[:, :, ds(t0, GRP)]
                V.tensor_tensor(aw, bank[slot][:].rearrange("p (t j) -> p j t", t=GRP), aw, ALU.mult).then_inc(s_gw, 1)

            onehots(0, 0)
            onehots(GRP, 1)
            with dve.Fori(0, T // GRP // 4 - 1) as it:
                for slot in range(4):
                    weigh(it * 4 + slot, it * (4 * GRP) + GRP * slot, slot)
                    onehots(it * (4 * GRP) + GRP * (slot + 2), slot)
            for slot in range(4):
                g = T // GRP - 4 + slot
                weigh(g, GRP * g, slot)
                if slot < 2:
                    onehots(GRP * (g + 2), slot)

            def a_low(j, slot):
                dve.wait_ge(s_Wh, j + 1)
                V.tensor_tensor(whl[:, slot, 1], act_w[:, ds(j, 1)].rearrange("p o t -> p (o t)"), whl[:, slot, 0].bitcast(F32),
                                ALU.subtract).then_inc(s_Wl, 1)

            a_low(0, 0)
            split_low(3, s_vl, (s_vh, 4), second=True)
            for k in range(1, 4):
                a_low(k, k)
            with dve.Fori(0, KEYS // 4 - 1) as it:
                for k in range(4):
                    split_low(k, s_vl, (s_vh, it * 4 + (k + 5)), second=True)
                    a_low(it * 4 + (k + 4), k)
            dve.wait_ge(s_fs, TT)
            V.tensor_scalar(stat[:, SS:SS + 2], stat[:, SS:SS + 2], 1.0 / D, EPS, ALU.mult, ALU.add).then_inc(s_fv, 1)
            dve.wait_ge(s_fd, 1)
            link(V.reciprocal(stat[:, RS:RS + 2], stat[:, RS:RS + 2]))
            for t in range(TT):
                V.scalar_tensor_tensor(fin[:, t].rearrange("p (a n) -> p a n", a=2), acc[:, 2 * t:2 * t + 2, :],
                                       stat[:, RS + t:RS + t + 1], gfin[:].rearrange("p (a n) -> p a n", a=2),
                                       ALU.mult, ALU.mult).then_inc(s_fin, 1)

        @block.tensor
        def _(pe):
            def transposes(k, src):
                pe.wait_ge(s_xs, k + 1)
                for c in range(DC):
                    for t in range(TT):
                        o = T * (c % 2) + P * t
                        last = pe.transpose(bank[c // 2][:, o:o + P], src[:, t, P * c:P * c + P], ident[:])
                    if c % 2:
                        last.then_inc(s_tr, 1)

            def unit(u, xin, fresh=None):
                pe.wait_ge(s_wl, u + 1)
                if u >= 2:
                    wevac(pe, u - 2)
                kind = UNITS[u][2]
                wh, wl = wsp[:, u % 2, 0], wsp[:, u % 2, 1]
                for k in range(2):
                    groups = ((0, LC), (LC, DC)) if kind == "groups" else ((0, DC),)
                    for g, (c0, c1) in enumerate(groups):
                        dst = acc[:, 2 * (u % 2) + k, WCOL * g:WCOL * g + WCOL]
                        for c in range(c0, c1):
                            if fresh and k == 0:
                                pe.wait_ge(fresh[0], fresh[1] + c + 1)
                            if kind == "cols":
                                q = slice(P * k, P * k + P)
                                ops = ((wh[:, c, q], xin[:, c, 0]), (wh[:, c, q], xin[:, c, 1]), (wl[:, c, q], xin[:, c, 0]))
                            else:
                                q = slice(P * k, P * k + P)
                                ops = ((xin[:, c, 0, q], wh[:, c]), (xin[:, c, 0, q], wl[:, c]), (xin[:, c, 1, q], wh[:, c]))
                            for n, (a, b) in enumerate(ops):
                                last = pe.matmul(dst, a, b, start=(c == c0 and n == 0), stop=(c == c1 - 1 and n == 2))
                last.then_inc(s_wmm, 1)

            def scores(h):
                half = slice(64 * (h % 2), 64 * (h % 2) + 64)
                b = bank[SCB + h % 2]
                if h >= 2:
                    pe.wait_ge(s_mx, h - 1)
                pe.matmul(b[:, 0:P], qt[half, h // 2, 0:P], ktt[half, h // 2, 0:P], start=True, stop=True)
                pe.matmul(b[:, P:3 * P], qt[half, h // 2, P:2 * P], ktt[half, h // 2, :], start=True, stop=True).then_inc(s_sc, 1)

            def probs_t(h):
                pe.wait_ge(s_pn, h + 1)
                if h >= 1:
                    pe.wait_ge(s_pe, h)
                p = pbuf[:, h % 2]
                pe.transpose(bank[TRB][:, 0:P], p[:, 0:P], ident[:])
                pe.transpose(bank[TRB][:, P:2 * P], p[:, P:2 * P], ident[:])
                pe.transpose(bank[TRB][:, 2 * P:3 * P], p[:, 2 * P:3 * P], ident[:]).then_inc(s_pt, 1)

            def head_pv(h):
                half = slice(64 * (h % 2), 64 * (h % 2) + 64)
                pe.wait_ge(s_pe, h + 1)
                if h >= 1:
                    pe.wait_ge(s_pve, h)
                vh = slice(DH * h, DH * h + DH)
                pe.matmul(bank[OUB][half, 0:T], v_sb[:, 0, vh], ptr[:, h % 2, 0:T], start=True, stop=False)
                pe.matmul(bank[OUB][half, P:T], v_sb[:, 1, vh], ptr[:, h % 2, T:T + P], start=False, stop=True).then_inc(s_pv, 1)

            pe.wait_ge(s_const, 7)
            transposes(0, xs)
            unit(0, xt, (s_tl, 0))
            unit(1, xt)
            transposes(1, mr)
            unit(2, xt)
            unit(3, xt)
            pe.wait_ge(s_bd, 64)
            pe.wait_ge(s_cv, CONV * LC)
            pe.wait_ge(s_tl, 2 * DC)
            for mch in range(LC):
                pe.matmul(bank[mch][:, 0:T], bd[:, 0, mch], cv_[:, mch], start=True, stop=True)
                pe.matmul(bank[mch][:, T:2 * T], bd[:, 1, mch], cv_[:, mch], start=True, stop=True).then_inc(s_lg, 1)
            for u in range(4, 9):
                unit(u, xt)
            wevac(pe, U_K + 1)
            pe.wait_ge(s_sg, LC)
            scores(0)
            for h in range(HEADS):
                if h + 1 < HEADS:
                    scores(h + 1)
                if h == 0:
                    unit(U_V + 1, xt)
                else:
                    unit(9 + h, memt)
                probs_t(h)
                if h == 1:
                    wevac(pe, U_V + 1)
                if h:
                    head_pv(h - 1)
            unit(U_OUT - 1, memt)
            head_pv(HEADS - 1)
            pe.wait_ge(s_pve, HEADS)
            pe.wait_ge(s_gss, 1 + LC)
            for g, sq in enumerate((r_, i_)):
                for t in range(TT):
                    for c in range(LC):
                        last = pe.matmul(bank[OUB][:, 2 * g + t:2 * g + t + 1], sq[:, c, P * t:P * t + P], ones[:, 0:1],
                                         start=(c == 0), stop=(c == LC - 1))
            last.then_inc(s_gmm, 1)
            unit(U_OUT, mixt, (s_gl, 0))
            for u in range(U_OUT + 1, U_CQ):
                unit(u, mixt)
            transposes(2, xs)

            def cross_scores(h):
                n = HEADS + h
                b = bank[SCB + n % 2]
                pe.wait_ge(s_ex, n - 1)
                for t in range(TT):
                    for c in range(2):
                        last = pe.matmul(b[:, T * t:T * t + T], qct[:, 2 * h + c, P * t:P * t + P], kct[:, 2 * h + c, :],
                                         start=(c == 0), stop=(c == 1))
                last.then_inc(s_sc, 1)

            def cross_probs_t(h):
                n = HEADS + h
                pe.wait_ge(s_pn, n + 1)
                pe.wait_ge(s_pe, n)
                for t in range(TT):
                    for k in range(TT):
                        last = pe.transpose(bank[TRB][:, T * k + P * t:T * k + P * t + P], pbuf[:, n % 2, T * t + P * k:T * t + P * k + P],
                                            ident[:])
                last.then_inc(s_pt, 1)

            def cross_pv(h):
                n = HEADS + h
                pe.wait_ge(s_pe, n + 1)
                if h:
                    pe.wait_ge(s_cl, h)
                for c in range(2):
                    for k in range(TT):
                        d0 = CDH * h + P * c
                        last = pe.matmul(bank[OUB][:, T * c:T * c + T], vc[:, k, d0:d0 + P], ptr[:, n % 2, T * k:T * k + T],
                                         start=(k == 0), stop=(k == TT - 1))
                last.then_inc(s_pv, 1)

            unit(U_CQ, xt, (s_tl, 2 * DC))
            unit(U_CQ + 1, xt)
            wevac(pe, U_CQ)
            cross_scores(0)
            unit(U_CQ + 2, xt)
            wevac(pe, U_CQ + 1)
            cross_scores(1)
            cross_probs_t(0)
            unit(U_CQ + 3, xt)
            cross_pv(0)
            cross_probs_t(1)
            wevac(pe, U_CQ + 3)
            cross_scores(2)
            cross_pv(1)
            cross_scores(3)
            cross_probs_t(2)
            cross_pv(2)
            cross_probs_t(3)
            cross_pv(3)
            pe.wait_ge(s_cl, CHEADS)
            for u in range(U_CO, U_PQ):
                unit(u, oct_)
            transposes(3, xs)
            unit(U_PQ, xt, (s_tl, 3 * DC))
            for u in range(U_PQ + 1, NU):
                unit(u, xt)
            pe.wait_ge(s_keys, 16)
            wevac(pe, NU - 1)
            for t in range(TT):
                for b in range(4):
                    n = 4 * t + b
                    if n >= 4:
                        pe.wait_ge(s_ke, n - 3)
                    for k in range(4):
                        hp = 4 * b + k
                        last = pe.matmul(bank[b][:, P * k:P * k + P], qpt[:, hp, P * t:P * t + P], keys[:, hp], start=True, stop=True)
                    last.then_inc(s_ks, 1)

            for t in range(TT):
                for n in range(2):
                    last = pe.matmul(acc[:, 2 * t + n], ident[:], xr[:, t, 512 * n:512 * n + 512], start=True, stop=False,
                                     skip_group_check=True)
            last.then_inc(s_seed, 1)

            def u_keys(it, first=False, last_pass=False):
                for k in range(4):
                    pe.wait_ge(s_ul, it * 4 + (k + 1))
                    if first:
                        pe.wait_ge(s_ke, 5 + k)
                    else:
                        pe.wait_ge(s_ua, it * 4 + (k - 3))
                    uh = eslot(k, 0, False).rearrange("p (c i) -> p c i", c=DC)
                    ul = eslot(k, 1, False).rearrange("p (c i) -> p c i", c=DC)
                    for c in range(DC):
                        pe.matmul(bank[k][:, 0:T], uh[:, c], xt[:, c, 0], start=(c == 0), stop=False)
                        pe.matmul(bank[k][:, 0:T], uh[:, c], xt[:, c, 1], start=False, stop=False)
                        last = pe.matmul(bank[k][:, 0:T], ul[:, c], xt[:, c, 0], start=False, stop=(c == DC - 1))
                    if last_pass and k < 3:
                        if k == 0:
                            pe.wait_ge(s_gr, 1)
                        for t in range(TT):
                            last = pe.transpose(bank[k][:, T + P * t:T + P * t + P], krow[:, k, t], ident[:])
                    last.then_inc(s_um, 1)

            u_keys(0, first=True)
            with pe.Fori(1, KEYS // 4 - 1) as it:
                u_keys(it)
            u_keys(KEYS // 4 - 1, last_pass=True)

            pe.wait_ge(s_ua, KEYS)
            pe.wait_ge(s_kte, 3)

            def route(it, slot, first=False):
                pe.wait_ge(s_oi, it * 4 + (slot + 1))
                pe.wait_ge(s_oja if slot % 2 else s_ojp, it * 2 + (slot // 2 + 1))
                if not first:
                    pe.wait_ge(s_gw, it * 4 + (slot - 3))
                for k in range(GRP):
                    last = pe.matmul(bank[slot][:, P * k:P * k + P], oh_i[:, slot % 2, k], oh_j(slot)[:, k], start=True, stop=True)
                last.then_inc(s_gm, 1)

            for slot in range(4):
                route(0, slot, first=True)
            with pe.Fori(1, T // GRP // 4) as it:
                for slot in range(4):
                    route(it, slot)

            def v_key(j, slot, last_key=False):
                pe.wait_ge(s_vl, j + 1)
                pe.wait_ge(s_Wl, j + 1)
                vh, vl = eslot(slot, 0, True), eslot(slot, 1, True)
                for t in range(TT):
                    ah, al = whl[:, slot, 0, P * t:P * t + P], whl[:, slot, 1, P * t:P * t + P]
                    for k, (a, b) in enumerate(((ah, vh), (ah, vl), (al, vh))):
                        for n in range(2):
                            last = pe.matmul(acc[:, 2 * t + n], a, b[:, 512 * n:512 * n + 512], start=False,
                                             stop=last_key and k == 2, skip_group_check=True)
                last.then_inc(s_vm, 1)

            with pe.Fori(0, KEYS // 4 - 1) as it:
                for slot in range(4):
                    v_key(it * 4 + slot, slot)
            for slot in range(4):
                v_key(KEYS - 4 + slot, slot, last_key=slot == 3)


def kernel(**inputs):
    import numpy as np
    import concourse.bacc as bacc
    from concourse.bass_utils import run_bass_kernel_spmd as run

    def chunks(a, n):
        return np.asarray(a).reshape(-1, n, P).transpose(2, 0, 1).reshape(P, -1)

    i = {k: np.asarray(a) for k, a in inputs.items()}
    par = np.concatenate([
        chunks(i["ln_mix_g"][0], DC), chunks(i["ln_mem_g"][0], DC), chunks(i["ln_cross_g"][0], DC), chunks(i["ln_ffn_g"][0], DC),
        chunks(i["gn_lru_g"][0], LC), chunks(i["gn_attn_g"][0], LC), chunks(i["conv_w"][0], LC), chunks(i["conv_b"][0], LC),
        chunks(i["lru_ba"][0], LC), chunks(i["lru_bx"][0], LC), chunks(i["lru_lambda"][0], LC)], axis=1)
    u_t = i["peer_u"][0].reshape(KEYS, KEYS // 2, 2, DC, P).transpose(1, 4, 2, 3, 0).reshape(KEYS // 2, P, 2, D)
    keys_t = i["peer_subkeys"][0].reshape(2 * PH, KEYS, P).transpose(2, 0, 1)
    arrays = {
        "x": i["x"][0], "mem": i["mem"][0], "par": par, "wa": i["lru_wa"][0], "wx": i["lru_wx"][0],
        "w_in": i["w_in"][0], "w_ck": i["w_ck"][0], "w_cv": i["w_cv"][0], "w_out": i["w_out"][0], "w_cq": i["w_cq"][0],
        "w_co": i["w_co"][0], "w_pq": i["peer_wq"][0], "keys_t": keys_t, "u_t": u_t, "v": i["peer_v"][0],
        "g_final": i["ln_final_g"],
    }
    arrays = {k: np.ascontiguousarray(a) for k, a in arrays.items()}
    nc = bacc.Bacc("TRN2", target_bir_lowering=False, num_devices=1)
    ap = {k: nc.dram_tensor(k, a.shape, mybir.dt.from_np(a.dtype), kind="ExternalInput").ap() for k, a in arrays.items()}
    out = nc.dram_tensor("out", (T, D), F32, kind="ExternalOutput").ap()
    w = {k: ap[k] for k in ("w_in", "w_ck", "w_cv", "w_out", "w_cq", "w_co", "w_pq")}
    build(nc, ap["x"], ap["mem"], ap["par"], ap["wa"], ap["wx"], w, ap["keys_t"], ap["u_t"], ap["v"], ap["g_final"], out)
    r = run(nc, [arrays], core_ids=[0])
    return r.results[0]["out"].reshape(1, T, D)
```

```python
from contextlib import ExitStack

import concourse.bass as bass
from concourse import mybir

F32 = mybir.dt.float32
F32R = mybir.dt.float32r
U32 = mybir.dt.uint32
ALU = mybir.AluOpType
ACT = mybir.ActivationFunctionType
X = mybir.AxisListType.X
ds = bass.ds

P = 128
T, D = 256, 1024
TT, DC = T // P, D // P
LC = 4
HEADS, DH = 8, 64
CHEADS, CDH = 4, 256
PH, TOPK, KEYS = 8, 16, 128
CONV = 4
EPS = 1e-6
NEG = -1e30
LOWEST = -3.0e38
WCOL = 256

PAR = {}
_at = 0
for _name, _n in (("ln_mix", DC), ("ln_mem", DC), ("ln_cross", DC), ("ln_ffn", DC), ("gn_lru", LC), ("gn_attn", LC),
                  ("conv_w", CONV * LC), ("conv_b", LC), ("ba", LC), ("bx", LC), ("lam", LC)):
    PAR[_name] = (_at, _n)
    _at += _n
NPAR = _at

UNITS = ([("w_in", WCOL * i, "cols") for i in range(8)] + [("w_in", WCOL * i, "rows") for i in range(8, 10)]
         + [("w_ck", WCOL * i, "cols") for i in range(4)] + [("w_cv", WCOL * i, "rows") for i in range(4)]
         + [("w_out", WCOL * i, "groups") for i in range(4)]
         + [("w_cq", WCOL * i, "cols") for i in range(4)] + [("w_co", WCOL * i, "rows") for i in range(4)]
         + [("w_pq", WCOL * i, "cols") for i in range(8)])
U_LRU, U_GATE, U_Q, U_K, U_V, U_CK, U_CV, U_OUT, U_CQ, U_CO, U_PQ = 0, 2, 4, 6, 8, 10, 14, 18, 22, 26, 30
NU = len(UNITS)
WRAW = 4
POOL_LOW = (U_CQ, U_PQ)
DVE_EVAC = set(range(U_OUT, U_CQ)) | set(range(U_CO, U_PQ))

JPB = 8
GRP = 4


def build(nc, x, mem, par, wa, wx, w, keys_t, u_t, v, g_final, out):
    ctx = ExitStack()
    with ctx:
        base = 16512

        def at(name, off, shape, dt=F32):
            return nc.alloc_sbuf_tensor_at(name, [P] + shape, dt, offset=base + off)

        def sem(name):
            return ctx.enter_context(nc.semaphore(name))

        K = 1024
        act_w = at("act_w", 0, [KEYS, T])
        xr = at("xr", 128 * K, [TT, D])
        xt = at("xt", 136 * K, [DC, 2, T], F32R)
        raw = at("raw", 152 * K, [2, 2, D])
        hl = at("hl", 168 * K, [2, 2, D], F32R)
        hl2 = at("hl2", 128 * K, [2, D], F32R)
        hl3v = at("hl3v", 136 * K, [2, D], F32R)
        oh_i1 = at("oh_i1", 136 * K, [2, GRP, P])
        gfin = at("gfin", 146 * K, [D])
        sqd = at("sqd", 140 * K, [3, GRP, P])
        fin = at("fin", 128 * K, [TT, D])
        m = 184 * K
        ident = at("ident", m, [P]); m += 512
        iota = at("iota", m, [P]); m += 512
        pars = at("pars", m, [NPAR]); m += 288
        ones = at("ones", m, [8]); m += 32
        stat = at("stat", m, [112]); m += 448
        kt3 = at("kt3", m, [3, T]); m += 3 * K
        krow = at("krow", m, [3, TT, P]); m += 3 * K
        oh_at = m
        hl3u = at("hl3u", m, [2, D], F32R)
        oh_i0 = at("oh_i0", m, [2, GRP, P])
        oh_j0 = at("oh_j0", m + 4 * K, [2, GRP, P])
        whl = at("whl", m, [4, 2, T], F32R)
        m += 8 * K
        oh_j1 = at("oh_j1", m, [2, GRP, P])
        cand = at("cand", m, [256])
        candw = at("candw", m + K, [256])
        rwork = at("rwork", m + 2 * K, [P])
        eq = at("eq", m + 2 * K + 512, [2, TOPK, TOPK])
        topv = at("topv", m + 4 * K + 512, [3, TOPK])
        topi = at("topi", m + 4 * K + 704, [3, TOPK], U32)
        posu = at("posu", m + 4 * K + 896, [2, TOPK], U32)
        posf = at("posf", m + 4 * K + 1024, [2, TOPK])
        topf = at("topf", m + 4 * K + 1152, [2, TOPK])
        m += 5 * K + 256
        mask = at("mask", m, [3 * P]); m += 1536
        assert base + m <= 229344
        wraw = at("wraw", 0, [WRAW, DC, WCOL])
        wsp = at("wsp", 32 * K, [2, 2, DC, WCOL], F32R)
        mr = at("mr", 64 * K, [TT, D])
        v_sb = at("v_sb", 64 * K, [TT, 512])
        ya = at("ya", 68 * K, [LC, T])
        memt = at("memt", 72 * K, [DC, 2, T], F32R)
        qct = at("qct", 72 * K, [DC, T])
        keys = at("keys", 80 * K, [2 * PH, KEYS])
        xs = at("xs", 88 * K, [TT, D])
        pbuf = at("pbuf", 88 * K, [2, 512])
        ptr = at("ptr", 92 * K, [2, 512])
        mixt = at("mixt", 96 * K, [DC, 2, T], F32R)
        oct_ = at("oct", 96 * K, [DC, 2, T], F32R)
        qpt = at("qpt", 96 * K, [2 * PH, T])
        kct = at("kct", 112 * K, [DC, T])
        bd = at("bd", 120 * K, [2, LC, P])
        vc = at("vc", 120 * K, [TT, D])
        srow = at("srow", 112 * K, [TT * PH, 2, KEYS])
        cx = at("cx", oh_at, [LC, T + CONV - 1])
        lru = at("lru", 152 * K, [8, LC, T])
        cv_, r_, i_, a_, th_, gel = (lru[:, k] for k in range(6))
        qt, ktt = lru[:, 6], lru[:, 7]

        def flat(ap):
            return ap.rearrange("p a b -> p (a b)")

        bank = [ctx.enter_context(nc.psum_tensor(f"bank{i}", [P, 512], F32)) for i in range(4, 8)]
        acc = ctx.enter_context(nc.psum_tensor("acc", [P, 4, 512], F32))

        SS, RS = 0, 16
        ND = 32
        SP = 48
        QS = 96
        WARM = 104
        GS = 72
        s_par, s_mem, s_bd, s_keys, s_gf, s_out = (sem(n) for n in (
            "s_par", "s_mem", "s_bd", "s_keys", "s_gf", "s_out"))
        s_x = [sem(f"s_x{i}") for i in range(TT)]
        s_w0, s_w0h, s_w0l, s_warm, s_yt = (sem(n) for n in ("s_w0_first", "s_w0_first_high", "s_w0_first_low", "s_warm", "s_y_tile0"))
        s_wr = [sem(f"s_wraw{i}") for i in range(WRAW)]
        s_wh, s_wl, s_wlp, s_wmm, s_weva, s_wevd = (sem(n) for n in ("s_w_high", "s_w_low", "s_w_low_pool", "s_w_mm", "s_w_evac_act", "s_w_evac_dve"))
        s_const = sem("s_const")
        s_sq, s_var, s_std, s_t0, s_res, s_xs, s_tr, s_th, s_tl = (sem(n) for n in (
            "s_squares", "s_variance", "s_deviation", "s_tile0_mm", "s_residual", "s_scaled", "s_transposed", "s_t_high", "s_t_low"))
        s_pool, s_dve, s_act = sem("s_pool_chain"), sem("s_dve_chain"), sem("s_act_chain")
        s_spe, s_spc = sem("s_softplus_exp"), sem("s_softplus_done")
        s_cv, s_lg, s_sg, s_at, s_b2, s_sqr, s_y = (sem(n) for n in (
            "s_conv", "s_lru_gate_mm", "s_lru_sigmoid", "s_lru_a_tanh", "s_lru_1ma2", "s_lru_sqrt", "s_lru_y"))
        s_gss, s_gad, s_gmm, s_gh, s_gl = (sem(n) for n in ("s_group_squares", "s_group_adds", "s_group_sums", "s_group_high", "s_group_low"))
        s_sc, s_mx, s_ex, s_pn, s_pt, s_pe, s_pv, s_pve = (sem(n) for n in (
            "s_scores", "s_att_max", "s_att_exp", "s_att_probs", "s_att_transposed", "s_att_probs_t", "s_att_pv", "s_att_out"))
        s_cl = sem("s_cross_low")
        s_ks, s_ke, s_rt, s_ge, s_gr, s_ktr, s_kte = (sem(n) for n in (
            "s_key_scores", "s_key_rows", "s_routed", "s_gate_exp", "s_gates", "s_key_transposed", "s_key_cols"))
        s_raw = [sem(f"s_raw{i}") for i in range(2)]
        s_uh, s_ul, s_um, s_ua = (sem(n) for n in ("s_u_high", "s_u_low", "s_u_mm", "s_u_gelu"))
        s_oi, s_gi, s_dif, s_ojd, s_oja, s_sqd, s_gm, s_gw = (sem(n) for n in (
            "s_onehot_i", "s_gated_i", "s_differences", "s_onehot_j_dve", "s_onehot_j_act", "s_sq_distance", "s_route_mm", "s_route_mul"))
        s_seed = sem("s_seed")
        s_vh, s_vl, s_Wh, s_Wl, s_vm = (sem(n) for n in ("s_v_high", "s_v_low", "s_a_high", "s_a_low", "s_v_mm"))
        s_fs, s_fv, s_fd, s_fin = (sem(n) for n in ("s_fin_squares", "s_fin_var", "s_fin_dev", "s_fin"))

        def pcol(name, c, n=1):
            o = PAR[name][0] + c
            return pars[:, o:o + n]

        def rows(ap):
            return ap.rearrange("(t p) d -> p t d", p=P)

        wd = {n: a.rearrange("(c p) n -> p c n", p=P) for n, a in w.items()}
        vd = v.rearrange("(i q j) d -> q i j d", i=KEYS, j=2)
        SCB, TRB, OUB = 0, 2, 3

        def wsplit(eng, u):
            if u in POOL_LOW:
                eng.wait_ge(s_wlp, POOL_LOW.index(u) + 1)
            else:
                eng.wait_ge(s_wl, u + 1 - sum(1 for k in POOL_LOW if k < u))

        def wevac(eng, u):
            if u in (U_CQ - 1, U_PQ - 1):
                eng.wait_ge(s_res, TT if u < U_CQ else 2 * TT)
            elif u in DVE_EVAC:
                eng.wait_ge(s_wevd, sum(1 for k in DVE_EVAC - {U_CQ - 1} if k <= u))
            else:
                eng.wait_ge(s_weva, sum(1 for k in range(u + 1) if k not in DVE_EVAC))

        def norm_count(n, t):
            return TT * n + t + 1 + (n > 1)

        def eslot(k, part, second):
            return (hl[:, 0], hl[:, 1], hl2, hl3v if second else hl3u)[k][:, part]

        def oh_i(slot):
            return (oh_i0, oh_i1)[slot // 2][:, slot % 2]

        def oh_j(slot):
            return (oh_j0, oh_j1)[slot // 2][:, slot % 2]

        block = ctx.enter_context(nc.Block())

        @block.sync
        def _(sp):
            for t in range(TT):
                sp.dma_start(xr[:, t], x[P * t:P * t + P, :]).then_inc(s_x[t], 16)
            sp.dma_start(pars[:], par).then_inc(s_par, 16)
            sp.dma_start(wraw[:, 0, 0:4], wd["w_in"][:, 0:4, 0:WCOL]).then_inc(s_w0, 16)
            sp.dma_start(wraw[:, 0, 4:8], wd["w_in"][:, 4:8, 0:WCOL]).then_inc(s_wr[0], 16)

            def unit(u):
                name, c0, _ = UNITS[u]
                if u >= WRAW:
                    wsplit(sp, u - WRAW)
                sp.dma_start(wraw[:, u % WRAW], wd[name][:, :, c0:c0 + WCOL]).then_inc(s_wr[u % WRAW], 16)

            unit(1)
            sp.dma_start(mr[:], rows(mem)).then_inc(s_mem, 16)
            for u in range(2, WRAW):
                unit(u)
            sp.wait_ge(s_const, 7)
            for k, src in enumerate((wa, wx)):
                for half in range(2):
                    q = slice(64 * half, 64 * half + 64)
                    sp.dma_start(bd[q, k, :, q], src[half::2].rearrange("m d e -> d m e")).then_inc(s_bd, 16)
            for u in range(WRAW, NU):
                unit(u)
                if u == U_PQ + 4:
                    sp.dma_start(keys[:], keys_t).then_inc(s_keys, 16)

            sp.wait_ge(s_pv, 8 + 4)
            for q in range(2):
                sp.dma_start(raw[:, q], u_t[q]).then_inc(s_raw[q], 16)
            with sp.Fori(1, KEYS // 4) as it:
                for q in range(2):
                    sp.wait_ge(s_ul, it * 4 - 4 + 2 * q + 2)
                    sp.dma_start(raw[:, q], u_t[ds(it * 2 + q, 1)].rearrange("o p j d -> (o p) j d")).then_inc(s_raw[q], 16)
            for q in range(2):
                sp.wait_ge(s_ul, KEYS - 4 + 2 * q + 2)
                sp.dma_start(raw[:, q], vd[q]).then_inc(s_raw[q], 16)
            sp.wait_ge(s_um, KEYS)
            sp.dma_start(gfin[:], g_final.rearrange("(o d) -> o d", o=1).broadcast_to([P, D])).then_inc(s_gf, 16)
            with sp.Fori(1, KEYS // 4) as it:
                for q in range(2):
                    sp.wait_ge(s_vl, it * 4 - 4 + 2 * q + 2)
                    sp.dma_start(raw[:, q], vd[ds(it * 2 + q, 1)].rearrange("o i j d -> (o i) j d")).then_inc(s_raw[q], 16)
            for t in range(TT):
                for n in range(2):
                    sp.wait_ge(s_fin, 2 * t + n + 1)
                    sp.dma_start(out[P * t:P * t + P, 512 * n:512 * n + 512], fin[:, t, 512 * n:512 * n + 512]).then_inc(s_out, 16)
            sp.wait_ge(s_out, 2 * 16 * TT)

        @block.gpsimd
        def _(pool):
            nc.gpsimd.memset(bd[:].rearrange("p a b c -> p (a b c)"), 0.0).then_inc(s_const, 1)
            nc.gpsimd.memset(ident[:], 0.0).then_inc(s_pool, 1)
            nc.gpsimd.memset(mask[:], 0.0).then_inc(s_pool, 1)
            pool.wait_ge(s_pool, 2)
            nc.gpsimd.affine_select(out=ident[:], in_=ident[:], compare_op=ALU.not_equal, fill=1.0, base=0,
                                    pattern=[[-1, P]], channel_multiplier=1).then_inc(s_const, 1)
            nc.gpsimd.affine_select(out=mask[:, 0:P], in_=mask[:, 0:P], compare_op=ALU.is_ge, fill=NEG, base=0,
                                    pattern=[[-1, P]], channel_multiplier=1).then_inc(s_const, 1)
            nc.gpsimd.affine_select(out=mask[:, P:3 * P], in_=mask[:, P:3 * P], compare_op=ALU.is_ge, fill=NEG, base=P,
                                    pattern=[[-1, 2 * P]], channel_multiplier=1).then_inc(s_const, 1)
            nc.gpsimd.iota(iota[:], pattern=[[1, P]], base=0, channel_multiplier=0,
                           allow_small_or_imprecise_dtypes=True).then_inc(s_const, 1)
            nc.gpsimd.memset(ones[:], 1.0).then_inc(s_const, 1)
            nc.gpsimd.memset(cx[:, :, 0:CONV - 1], 0.0).then_inc(s_const, 1)
            def add(dst, src):
                return nc.gpsimd.tensor_tensor(dst, dst, src, ALU.add)

            pool.wait_ge(s_gss, 1)
            add(r_[:, 0], r_[:, 1]).then_inc(s_gad, 1)
            add(r_[:, 2], r_[:, 3]).then_inc(s_gad, 1)
            pool.wait_ge(s_gad, 2)
            add(r_[:, 0], r_[:, 2]).then_inc(s_gad, 1)
            for c in range(1, LC):
                pool.wait_ge(s_gss, 1 + c + 1)
                pool.wait_ge(s_gad, 2 + c)
                add(i_[:, 0], i_[:, c]).then_inc(s_gad, 1)

            for u in POOL_LOW:
                pool.wait_ge(s_wh, u + 1)
                nc.gpsimd.tensor_tensor(wsp[:, u % 2, 1], wraw[:, u % WRAW], wsp[:, u % 2, 0].bitcast(F32),
                                        ALU.subtract).then_inc(s_wlp, 1)

            pool.wait_ge(s_kte, 3)
            pool.wait_ge(s_um, KEYS)

            def gate_rows(g, t0, slot):
                pool.wait_ge(s_oi, g + 1)
                nc.gpsimd.tensor_tensor(oh_i(slot), oh_i(slot), kt3[:, 2, ds(t0, GRP)].unsqueeze(2).broadcast_to([P, GRP, P]),
                                        ALU.mult).then_inc(s_gi, 1)

            def differences(t0, seen=None):
                if seen is not None:
                    pool.wait_ge(s_oja, seen)
                nc.gpsimd.tensor_tensor(sqd[:, 0], kt3[:, 1, ds(t0, GRP)].unsqueeze(2).broadcast_to([P, GRP, P]),
                                        iota[:].unsqueeze(1).broadcast_to([P, GRP, P]), ALU.subtract).then_inc(s_dif, 1)

            differences(0)
            with pool.Fori(0, T // GRP // 4 - 1) as it:
                for slot in range(4):
                    gate_rows(it * 4 + slot, it * (4 * GRP) + GRP * slot, slot)
                    if slot == 1:
                        differences(it * (4 * GRP) + 4 * GRP, it * 3 + 1)
            for slot in range(4):
                g = T // GRP - 4 + slot
                gate_rows(g, GRP * g, slot)

        @block.scalar
        def _(act):
            chain = [0]

            def link(ins):
                chain[0] += 1
                ins.then_inc(s_act, 1)
                act.wait_ge(s_act, chain[0])

            def w_high(u):
                act.wait_ge(s_wr[u % WRAW], 16 * (u // WRAW + 1))
                if u >= 2:
                    act.wait_ge(s_wmm, u - 1)
                nc.scalar.activation(wsp[:, u % 2, 0], wraw[:, u % WRAW], ACT.Copy).then_inc(s_wh, 1)

            def unit(u):
                if u + 2 < NU:
                    w_high(u + 2)
                if u in DVE_EVAC:
                    return
                act.wait_ge(s_wmm, u + 1)
                dst = unit_dst(u)
                for k in range(2):
                    last = nc.scalar.activation(dst(k), acc[:, 2 * (u % 2) + k, 0:WCOL], ACT.Copy)
                last.then_inc(s_weva, 1)

            def warm_sqrt():
                nc.scalar.activation(stat[:, WARM + 1:WARM + 2], stat[:, WARM:WARM + 1], ACT.Sqrt)

            def tile_deviation(n, t):
                act.wait_ge(s_var, norm_count(n, t))
                nc.scalar.activation(stat[:, RS + 2 * n + t:RS + 2 * n + t + 1], stat[:, SS + 2 * n + t:SS + 2 * n + t + 1],
                                     ACT.Sqrt).then_inc(s_std, 1)

            def squares(n, t, src, junk):
                nc.scalar.activation(junk[:, t], src[:, t], ACT.Square,
                                     accum_out=stat[:, SS + 2 * n + t:SS + 2 * n + t + 1]).then_inc(s_sq, 1)

            def split0(c0, c1):
                return nc.scalar.activation(wsp[:, 0, 0, c0:c1], wraw[:, 0, c0:c1], ACT.Copy)

            def t_high(k, gain, dst):
                for c in range(DC):
                    if c % 2 == 0:
                        act.wait_ge(s_tr, 4 * k + c // 2 + 1)
                    nc.scalar.activation(dst[:, c, 0], bank[c // 2][:, T * (c % 2):T * (c % 2) + T], ACT.Copy,
                                         scale=pcol(gain, c)).then_inc(s_th, 1)

            def unit_dst(u):
                def cols(dst, u0):
                    return lambda k: dst[:, 2 * (u - u0) + k]

                def token_rows(dst, u0):
                    return lambda k: dst[:, k, WCOL * (u - u0):WCOL * (u - u0) + WCOL]

                if u < U_GATE:
                    return lambda k: cx[:, 2 * u + k, CONV - 1:]
                for u1, f, dst, u0 in ((U_Q, cols, gel, U_GATE), (U_K, cols, qt, U_Q), (U_V, cols, ktt, U_K),
                                       (U_CK, token_rows, v_sb, U_V), (U_CV, cols, kct, U_CK), (U_OUT, token_rows, vc, U_CV),
                                       (U_CO, cols, qct, U_CQ), (NU, cols, qpt, U_PQ)):
                    if u < u1:
                        return f(dst, u0)

            act.wait_ge(s_warm, 1)
            warm_sqrt()
            for t in range(TT):
                act.wait_ge(s_x[t], 16)
                squares(0, t, xr, xs)
                tile_deviation(0, t)
            act.wait_ge(s_w0, 16)
            split0(0, 4).then_inc(s_w0h, 1)
            act.wait_ge(s_wr[0], 16)
            split0(4, 8).then_inc(s_wh, 1)
            act.wait_ge(s_par, 16)
            t_high(0, "ln_mix", xt)
            w_high(1)
            act.wait_ge(s_mem, 16)
            for t in range(TT):
                squares(1, t, mr, kct[:].rearrange("p (t c) n -> p t (c n)", t=TT))
                tile_deviation(1, t)
            act.wait_ge(s_const, 7)
            for u in (0, 1):
                unit(u)
            act.wait_ge(s_weva, 2)
            for mch in range(LC):
                nc.scalar.activation(cv_[:, mch], cx[:, mch, 0:T], ACT.Identity, scale=pcol("conv_w", mch),
                                     bias=pcol("conv_b", mch)).then_inc(s_cv, 1)
            t_high(1, "ln_mem", memt)
            act.wait_ge(s_spe, 1)
            nc.scalar.activation(stat[:, SP + 4:SP + 8], stat[:, SP:SP + 4], ACT.Exp, scale=-1.0).then_inc(s_spc, 1)
            for u in (2, 3):
                unit(u)
            for mch in range(LC):
                act.wait_ge(s_lg, mch + 1)
                nc.scalar.activation(r_[:, mch], bank[mch][:, 0:T], ACT.Sigmoid, bias=pcol("ba", mch))
                nc.scalar.activation(i_[:, mch], bank[mch][:, T:2 * T], ACT.Sigmoid, bias=pcol("bx", mch)).then_inc(s_sg, 1)
            for u in (4, 5):
                unit(u)
            act.wait_ge(s_spc, 2)
            act.wait_ge(s_sg, LC)
            for mch in range(LC):
                nc.scalar.activation(a_[:, mch], r_[:, mch], ACT.Exp, scale=stat[:, SP + 20 + mch:SP + 21 + mch])
                last = nc.scalar.activation(th_[:, mch], r_[:, mch], ACT.Tanh, scale=stat[:, SP + 20 + mch:SP + 21 + mch])
            last.then_inc(s_at, 1)
            for u in (6, 7):
                unit(u)
            act.wait_ge(s_weva, 4)
            nc.scalar.activation(gel[:], gel[:], ACT.Gelu).then_inc(s_at, 1)
            act.wait_ge(s_b2, 1)
            nc.scalar.activation(th_[:], th_[:], ACT.Sqrt, scale=-1.0).then_inc(s_sqr, 1)
            unit(8)

            def group_high(c):
                src, gain = (a_, "gn_lru") if c < LC else (ya, "gn_attn")
                nc.scalar.activation(mixt[:, c, 0], src[:, c % LC], ACT.Copy, scale=pcol(gain, c % LC)).then_inc(s_gh, 1)

            def softmax_exp(n, scale, widths, src):
                slot = n % 2
                st = ND + 6 * slot
                act.wait_ge(s_mx, n + 1)
                o = 0
                for t, wdt in enumerate(widths):
                    last = nc.scalar.activation(pbuf[:, slot, o:o + wdt], src[:, o:o + wdt], ACT.Exp, scale=scale,
                                                bias=stat[:, st + t:st + t + 1], accum_out=stat[:, st + 2 + t:st + 3 + t])
                    o += wdt
                last.then_inc(s_ex, 1)

            def probs_t(n, cols):
                slot = n % 2
                act.wait_ge(s_pt, n + 1)
                if n >= 2:
                    act.wait_ge(s_pv, n - 1)
                nc.scalar.activation(ptr[:, slot, 0:cols], bank[TRB][:, 0:cols], ACT.Copy).then_inc(s_pe, 1)

            for h in range(HEADS):
                softmax_exp(h, 1.0, (P, 2 * P), pbuf[:, h % 2])
                unit(9 + h)
                probs_t(h, 3 * P)
                if h == 2:
                    act.wait_ge(s_y, 1)
                    nc.scalar.activation(r_[:], a_[:], ACT.Square).then_inc(s_gss, 1)
                    for c in range(LC):
                        group_high(c)
            for c in range(LC, DC):
                act.wait_ge(s_pve, 2 * (c - LC) + 2)
                group_high(c)
                nc.scalar.activation(i_[:, c - LC], ya[:, c - LC], ACT.Square).then_inc(s_gss, 1)
            unit(U_OUT - 1)
            act.wait_ge(s_var, 5)
            nc.scalar.activation(stat[:, RS + 12:RS + 16], stat[:, SS + 12:SS + 16], ACT.Sqrt).then_inc(s_std, 1)

            def residual_units(u0, n):
                def quarter(t, q):
                    c = QS + 4 * t + q
                    return nc.scalar.activation(xs[:, t, WCOL * q:WCOL * q + WCOL], xr[:, t, WCOL * q:WCOL * q + WCOL],
                                                ACT.Square, accum_out=stat[:, c:c + 1])

                for q in range(3):
                    unit(u0 + q)
                    act.wait_ge(s_wevd, 3 * (n - 2) + q + 1)
                    for t in range(TT):
                        last = quarter(t, q)
                    last.then_inc(s_sq, 1)
                for t in range(TT):
                    act.wait_ge(s_res, TT * (n - 2) + t + 1)
                    quarter(t, 3).then_inc(s_sq, 1)
                    tile_deviation(n, t)

            def after_norm(u, k, gain):
                act.wait_ge(s_wr[(u + 2) % WRAW], 16 * ((u + 2) // WRAW + 1))
                act.wait_ge(s_wmm, u + 1)
                nc.scalar.activation(wsp[:, u % 2, 0, 0:4], wraw[:, (u + 2) % WRAW, 0:4], ACT.Copy)
                t_high(k, gain, xt)
                nc.scalar.activation(wsp[:, u % 2, 0, 4:8], wraw[:, (u + 2) % WRAW, 4:8], ACT.Copy).then_inc(s_wh, 1)

            residual_units(U_OUT, 2)
            after_norm(U_CQ - 1, 2, "ln_cross")

            def cross_exp(h):
                n = HEADS + h
                softmax_exp(n, CDH ** -0.5, (T, T), bank[SCB + n % 2])

            def cross_out(h):
                act.wait_ge(s_pv, HEADS + h + 1)
                nc.scalar.activation(oct_[:, 2 * h:2 * h + 2, 0], bank[OUB][:].rearrange("p (c t) -> p c t", c=2),
                                     ACT.Copy).then_inc(s_gh, 1)

            unit(U_CQ)
            unit(U_CQ + 1)
            cross_exp(0)
            unit(U_CQ + 2)
            probs_t(HEADS, 2 * T)
            cross_exp(1)
            unit(U_CQ + 3)
            cross_out(0)
            probs_t(HEADS + 1, 2 * T)
            cross_exp(2)
            cross_out(1)
            cross_exp(3)
            probs_t(HEADS + 2, 2 * T)
            cross_out(2)
            probs_t(HEADS + 3, 2 * T)
            cross_out(3)
            residual_units(U_CO, 3)
            after_norm(U_PQ - 1, 3, "ln_ffn")
            for u in range(U_PQ, NU):
                unit(u)
            sr = srow[:].rearrange("p (t h) a k -> p t (h a k)", t=TT)
            for n in range(8):
                act.wait_ge(s_ks, n + 1)
                nc.scalar.activation(sr[:, n // 4, 512 * (n % 4):512 * (n % 4) + 512], bank[n % 4][:], ACT.Copy).then_inc(s_ke, 1)

            def split_high(k, landed, free, ready, second=False):
                if landed is not None:
                    act.wait_ge(s_raw[k // 2], landed)
                if free is not None:
                    act.wait_ge(*free)
                nc.scalar.activation(eslot(k, 0, second), raw[:, k // 2, k % 2], ACT.Copy).then_inc(ready, 1)

            def gelu(j, k):
                act.wait_ge(s_um, j + 1)
                nc.scalar.activation(act_w[:, ds(j, 1)].rearrange("p o t -> p (o t)"), bank[k % 4][:, 0:T], ACT.Gelu).then_inc(s_ua, 1)

            act.wait_ge(s_pv, HEADS + CHEADS)
            for k in range(4):
                split_high(k, 16 if k % 2 == 0 else None, (s_seed, 1) if k == 2 else None, s_uh)
            base16 = 16 * (KEYS // 4)

            with act.Fori(0, KEYS // JPB - 1) as it:
                for jj in range(JPB):
                    j = it * JPB + jj
                    if jj == JPB - 1:
                        act.wait_ge(s_rt, it + 1)
                    gelu(j, jj)
                    split_high(jj % 4, (it * 2 + (jj // 4 + 2)) * 16 if jj % 2 == 0 else None, (s_um, j + 1), s_uh)
            act.wait_ge(s_rt, TT * PH)
            nc.scalar.activation(krow[:, 2], krow[:, 2], ACT.Exp).then_inc(s_ge, 1)
            for jj in range(JPB):
                j = KEYS - JPB + jj
                if jj < 4:
                    split_high(jj, base16 if jj % 2 == 0 else None, (s_um, j + 1), s_uh)
                elif jj < 7:
                    split_high(jj - 4, base16 + 16 if jj % 2 == 0 else None, (s_um, j + 1), s_vh, second=True)
                gelu(j, jj)
                if 4 <= jj < 7:
                    nc.scalar.activation(kt3[:, jj - 4], bank[jj - 4][:, T:2 * T], ACT.Copy).then_inc(s_kte, 1)

            def onehots(it, n, g, t0, slot, first):
                if not first:
                    act.wait_ge(s_gm, g - 3)
                if slot == 0:
                    act.wait_ge(s_dif, it + 1)
                    last = nc.scalar.activation(sqd[:, 0], sqd[:, 0], ACT.Square)
                for k in range(GRP if slot else 0):
                    last = nc.scalar.activation(sqd[:, slot, k], iota[:], ACT.Square, scale=-1.0, bias=kt3[:, 1, ds(t0 + k, 1)])
                last.then_inc(s_sqd, 1)
                act.wait_ge(s_sqd, n + 1)
                nc.scalar.activation(oh_j(slot), sqd[:, slot], ACT.Relu, scale=-1.0, bias=ones[:, 0:1]).then_inc(s_oja, 1)

            act.wait_ge(s_kte, 3)
            for slot in range(3):
                onehots(0, slot, slot, GRP * slot, slot, True)
            with act.Fori(1, T // GRP // 4) as it:
                for slot in range(3):
                    onehots(it, it * 3 + slot, it * 4 + slot, it * (4 * GRP) + GRP * slot, slot, False)

            def a_high(j, slot):
                nc.scalar.activation(whl[:, slot, 0], act_w[:, ds(j, 1)].rearrange("p o t -> p (o t)"), ACT.Copy).then_inc(s_Wh, 1)

            act.wait_ge(s_gw, T // GRP)
            for k in range(4):
                a_high(k, k)
            split_high(3, None, None, s_vh, second=True)
            with act.Fori(0, KEYS // 4 - 1) as it:
                for k in range(4):
                    split_high(k, (it + 2) * 16 + base16 if k % 2 == 0 else None, (s_vm, it * 4 + (k + 1)), s_vh, second=True)
                    a_high(it * 4 + (k + 4), k)
            warm_sqrt()
            for t in range(TT):
                act.wait_ge(*((s_yt, 1) if t == 0 else (s_vm, KEYS)))
                nc.scalar.activation(xs[:, t].rearrange("p (a n) -> p a n", a=2), acc[:, 2 * t:2 * t + 2, :], ACT.Square,
                                     accum_out=stat[:, SS + t:SS + t + 1]).then_inc(s_fs, 1)
                act.wait_ge(s_fv, t + 1)
                nc.scalar.activation(stat[:, RS + t:RS + t + 1], stat[:, SS + t:SS + t + 1], ACT.Sqrt).then_inc(s_fd, 1)

        @block.vector
        def _(dve):
            V = nc.vector
            chain = [0]

            def link(ins):
                chain[0] += 1
                ins.then_inc(s_dve, 1)
                dve.wait_ge(s_dve, chain[0])

            def w_low(u):
                dve.wait_ge(s_wh, u + 1)
                V.tensor_tensor(wsp[:, u % 2, 1], wraw[:, u % WRAW], wsp[:, u % 2, 0].bitcast(F32), ALU.subtract).then_inc(s_wl, 1)

            def unit(u):
                if u + 2 < NU:
                    w_low(u + 2)

            def tile_norm(n, t, src, dst):
                dve.wait_ge(s_sq, TT * n + t + 1 if n < 2 else 2 * TT + 5 * (n - 2) + 3 + t + 1)
                ss = stat[:, SS + 2 * n + t:SS + 2 * n + t + 1]
                if n >= 2:
                    link(V.tensor_reduce(ss, stat[:, QS + 4 * t:QS + 4 * t + 4], X, ALU.add))
                V.tensor_scalar(ss, ss, 1.0 / D, EPS, ALU.mult, ALU.add).then_inc(s_var, 1)
                dve.wait_ge(s_std, norm_count(n, t))
                rd = stat[:, RS + 2 * n + t:RS + 2 * n + t + 1]
                link(V.reciprocal(rd, rd))
                V.tensor_scalar(dst[:, t], src[:, t], rd, None, ALU.mult).then_inc(s_xs, 1)

            def t_low(k, gain, dst):
                for c in range(DC):
                    dve.wait_ge(s_th, DC * k + c + 2 - c % 2)
                    V.scalar_tensor_tensor(dst[:, c, 1], bank[c // 2][:, T * (c % 2):T * (c % 2) + T], pcol(gain, c),
                                           dst[:, c, 0].bitcast(F32), ALU.mult, ALU.subtract).then_inc(s_tl, 1)

            V.memset(stat[:, WARM:WARM + 1], 1.0).then_inc(s_warm, 1)
            for t in range(TT):
                tile_norm(0, t, xr, xs)
            dve.wait_ge(s_par, 16)
            lam = pcol("lam", 0, LC)
            c4 = lambda k: stat[:, SP + 4 * k:SP + 4 * k + 4]
            V.scalar_tensor_tensor(c4(0), lam, -1.0, lam, ALU.mult, ALU.max).then_inc(s_spe, 1)

            def split0(c0, c1):
                return V.tensor_tensor(wsp[:, 0, 1, c0:c1], wraw[:, 0, c0:c1], wsp[:, 0, 0, c0:c1].bitcast(F32), ALU.subtract)

            dve.wait_ge(s_w0h, 1)
            split0(0, 4).then_inc(s_w0l, 1)
            dve.wait_ge(s_wh, 1)
            split0(4, 8).then_inc(s_wl, 1)
            t_low(0, "ln_mix", xt)
            w_low(1)
            for t in range(TT):
                tile_norm(1, t, mr, mr)
            unit(0)
            unit(1)
            for s in range(1, CONV):
                dve.wait_ge(s_cv, LC * s)
                for mch in range(LC):
                    V.scalar_tensor_tensor(cv_[:, mch], cx[:, mch, s:s + T], pcol("conv_w", LC * s + mch), cv_[:, mch],
                                           ALU.mult, ALU.add).then_inc(s_cv, 1)
            t_low(1, "ln_mem", memt)
            unit(2)
            unit(3)
            dve.wait_ge(s_spc, 1)
            e, z, z2, q, sp8 = c4(1), c4(2), c4(3), c4(4), c4(5)
            link(V.tensor_scalar(z, e, 2.0, None, ALU.add))
            link(V.reciprocal(z, z))
            link(V.tensor_tensor(z, z, e, ALU.mult))
            link(V.tensor_tensor(z2, z, z, ALU.mult))
            link(V.tensor_scalar(q, z2, 1.0 / 17, None, ALU.mult))
            for n in (15, 13, 11, 9, 7, 5, 3):
                link(V.scalar_tensor_tensor(q, q, 1.0 / n, z2, ALU.add, ALU.mult))
            link(V.scalar_tensor_tensor(q, q, 1.0, z, ALU.add, ALU.mult))
            link(V.tensor_scalar(z, lam, -1.0, 0.0, ALU.mult, ALU.max))
            link(V.scalar_tensor_tensor(sp8, q, 2.0, z, ALU.mult, ALU.add))
            V.tensor_scalar(sp8, sp8, -8.0, None, ALU.mult).then_inc(s_spc, 1)
            unit(4)
            unit(5)
            dve.wait_ge(s_sg, LC)
            dve.wait_ge(s_cv, CONV * LC)
            link(V.tensor_tensor(i_[:], i_[:], cv_[:], ALU.mult))
            unit(6)
            dve.wait_ge(s_at, 1)
            link(V.tensor_tensor(r_[:], a_[:], a_[:], ALU.mult))
            V.scalar_tensor_tensor(th_[:], r_[:], 1.0, th_[:], ALU.add, ALU.mult).then_inc(s_b2, 1)
            unit(7)
            dve.wait_ge(s_sqr, 1)
            link(V.tensor_tensor(i_[:], i_[:], th_[:], ALU.mult))
            for mch in range(LC):
                last = V.tensor_tensor_scan(r_[:, mch], a_[:, mch], i_[:, mch], 0.0, ALU.mult, ALU.add)
            link(last)

            def normalise(n, widths):
                slot = n % 2
                st = ND + 6 * slot
                dve.wait_ge(s_ex, n + 1)
                link(V.reciprocal(stat[:, st + 4:st + 6], stat[:, st + 2:st + 4]))
                o = 0
                for t, wdt in enumerate(widths):
                    last = V.tensor_scalar(pbuf[:, slot, o:o + wdt], pbuf[:, slot, o:o + wdt], stat[:, st + 4 + t:st + 5 + t],
                                           None, ALU.mult)
                    o += wdt
                last.then_inc(s_pn, 1)

            def masked_max(h):
                slot = h % 2
                dve.wait_ge(s_sc, h + 1)
                if h >= 2:
                    dve.wait_ge(s_pt, h - 1)
                link(V.scalar_tensor_tensor(pbuf[:, slot, 0:3 * P], bank[SCB + slot][:, 0:3 * P], DH ** -0.5, mask[:],
                                            ALU.mult, ALU.add))
                V.tensor_reduce(stat[:, ND + 6 * slot:ND + 6 * slot + 1], pbuf[:, slot, 0:P], X, ALU.max, negate=True)
                V.tensor_reduce(stat[:, ND + 6 * slot + 1:ND + 6 * slot + 2], pbuf[:, slot, P:3 * P], X, ALU.max,
                                negate=True).then_inc(s_mx, 1)

            def head_out(h):
                half = slice(64 * (h % 2), 64 * (h % 2) + 64)
                dve.wait_ge(s_pv, h + 1)
                V.tensor_copy(ya[half, h // 2], bank[OUB][half, 0:T]).then_inc(s_pve, 1)

            masked_max(0)
            unit(8)

            def group_low(c):
                src, gain = (a_, "gn_lru") if c < LC else (ya, "gn_attn")
                dve.wait_ge(s_gh, c + 1)
                V.scalar_tensor_tensor(mixt[:, c, 1], src[:, c % LC], pcol(gain, c % LC), mixt[:, c, 0].bitcast(F32),
                                       ALU.mult, ALU.subtract).then_inc(s_gl, 1)

            for h in range(HEADS):
                if h == 0:
                    normalise(h, (P, 2 * P))
                    masked_max(h + 1)
                    dve.wait_ge(s_at, 2)
                    V.tensor_tensor(a_[:], r_[:], gel[:], ALU.mult).then_inc(s_y, 1)
                else:
                    if h + 1 < HEADS:
                        masked_max(h + 1)
                    normalise(h, (P, 2 * P))
                unit(9 + h)
                if h:
                    head_out(h - 1)
                if 3 <= h < 7:
                    group_low(h - 3)
            for c in range(LC, DC - 1):
                group_low(c)
            head_out(HEADS - 1)
            group_low(DC - 1)
            unit(U_OUT - 1)
            dve.wait_ge(s_gmm, 1)
            V.tensor_scalar(stat[:, SS + 12:SS + 16], bank[OUB][:, T:T + 4], 1.0 / 512, EPS, ALU.mult, ALU.add).then_inc(s_var, 1)
            dve.wait_ge(s_std, 5)
            rs = stat[:, RS + 12:RS + 16]
            link(V.reciprocal(rs, rs))

            def out_residual(u, t):
                c0 = WCOL * (u - U_OUT)
                xc = xr[:, t, c0:c0 + WCOL]
                for g in range(2):
                    last = V.scalar_tensor_tensor(xc, acc[:, 2 * (u % 2) + t, WCOL * g:WCOL * g + WCOL],
                                                  rs[:, 2 * g + t:2 * g + t + 1], xc, ALU.mult, ALU.add)
                    if g == 0:
                        link(last)
                return last

            def cross_residual(u, t):
                c0 = WCOL * (u - U_CO)
                xc = xr[:, t, c0:c0 + WCOL]
                return V.tensor_tensor(xc, acc[:, 2 * (u % 2) + t, 0:WCOL], xc, ALU.add)

            def residual_units(u0, n, residual):
                for u in range(u0, u0 + 3):
                    dve.wait_ge(s_wmm, u + 1)
                    residual(u, 0)
                    residual(u, 1).then_inc(s_wevd, 1)
                    if u < u0 + 2:
                        unit(u)
                dve.wait_ge(s_t0, n - 1)
                residual(u0 + 3, 0).then_inc(s_res, 1)
                tile_norm(n, 0, xr, xs)
                dve.wait_ge(s_wmm, u0 + 4)
                residual(u0 + 3, 1).then_inc(s_res, 1)
                tile_norm(n, 1, xr, xs)

            residual_units(U_OUT, 2, out_residual)
            t_low(2, "ln_cross", xt)
            unit(U_CQ - 1)

            def cross_max(h):
                n = HEADS + h
                st = ND + 6 * (n % 2)
                dve.wait_ge(s_sc, n + 1)
                link(V.tensor_reduce(stat[:, st:st + 2], bank[SCB + n % 2][:].rearrange("p (t k) -> p t k", t=TT), X, ALU.max))
                dve.wait_ge(s_pt, n - 1)
                V.tensor_scalar(stat[:, st:st + 2], stat[:, st:st + 2], -CDH ** -0.5, None, ALU.mult).then_inc(s_mx, 1)
                normalise(n, (T, T))

            def cross_low(h):
                dve.wait_ge(s_gh, DC + h + 1)
                V.tensor_tensor(oct_[:, 2 * h:2 * h + 2, 1], bank[OUB][:].rearrange("p (c t) -> p c t", c=2),
                                oct_[:, 2 * h:2 * h + 2, 0].bitcast(F32), ALU.subtract).then_inc(s_cl, 1)

            unit(U_CQ)
            unit(U_CQ + 1)
            cross_max(0)
            unit(U_CQ + 2)
            cross_max(1)
            unit(U_CQ + 3)
            cross_low(0)
            cross_max(2)
            cross_low(1)
            cross_max(3)
            cross_low(2)
            cross_low(3)
            residual_units(U_CO, 3, cross_residual)
            t_low(3, "ln_ffn", xt)
            unit(U_PQ - 1)
            for u in range(U_PQ, NU):
                unit(u)

            def split_low(k, ready, have, second=False):
                dve.wait_ge(*have)
                V.tensor_tensor(eslot(k, 1, second), raw[:, k // 2, k % 2], eslot(k, 0, second).bitcast(F32),
                                ALU.subtract).then_inc(ready, 1)

            ROUTE_LINKS = 20
            chain0 = chain[0]

            def route_pass(it, part):
                n = [5 * part]

                def rlink(ins):
                    n[0] += 1
                    ins.then_inc(s_dve, 1)
                    dve.wait_ge(s_dve, it * ROUTE_LINKS + (chain0 + n[0]))

                def best16(src, work, k):
                    rlink(V.max(topv[:, k, 0:8], src))
                    rlink(V.match_replace(work, topv[:, k, 0:8], src, LOWEST))
                    rlink(V.max(topv[:, k, 8:16], work))
                    V.max_index(topi[:, k, 0:8], topv[:, k, 0:8], src)
                    rlink(V.max_index(topi[:, k, 8:16], topv[:, k, 8:16], work))

                if part < 2:
                    best16(srow[:, ds(it, 1), part].rearrange("p o k -> p (o k)"), rwork[:], part)
                    rlink(V.tensor_copy(topf[:, part], topi[:, part]))
                elif part == 2:
                    rlink(V.tensor_tensor(cand[:].rearrange("p (a b) -> p a b", a=TOPK),
                                          topv[:, 0].unsqueeze(2).broadcast_to([P, TOPK, TOPK]),
                                          topv[:, 1].unsqueeze(1).broadcast_to([P, TOPK, TOPK]), ALU.add))
                    best16(cand[:], candw[:], 2)
                else:
                    V.tensor_scalar(posu[:, 0], topi[:, 2], 4, None, ALU.logical_shift_right)
                    rlink(V.tensor_scalar(posu[:, 1], topi[:, 2], 15, None, ALU.bitwise_and))
                    rlink(V.tensor_copy(flat(posf[:]), flat(posu[:])))
                    rlink(V.tensor_tensor(eq[:].rearrange("p a k b -> p (a k) b"),
                                          flat(posf[:]).unsqueeze(2).broadcast_to([P, 2 * TOPK, TOPK]),
                                          iota[:, 0:TOPK].unsqueeze(1).broadcast_to([P, 2 * TOPK, TOPK]), ALU.is_equal))
                    rlink(V.tensor_tensor(eq[:], eq[:], topf[:].unsqueeze(2).broadcast_to([P, 2, TOPK, TOPK]), ALU.mult))
                    kr = krow[:].rearrange("p a t (h k) -> p a (t h) k", k=TOPK)
                    rlink(V.tensor_reduce(kr[:, 0:2, ds(it, 1)].rearrange("p a o k -> p a (o k)"), eq[:], X, ALU.add))
                    V.tensor_scalar(kr[:, 2, ds(it, 1)], topv[:, 2:3], topv[:, 2, 0:1], None, ALU.subtract).then_inc(s_rt, 1)

            for k in range(4):
                split_low(k, s_ul, (s_uh, k + 1))
            dve.wait_ge(s_ke, 8)
            parts = 0
            for j in range(KEYS - 1):
                if j < KEYS - 4:
                    split_low(j % 4, s_ul, (s_uh, j + 5))
                else:
                    split_low(j % 4, s_vl, (s_vh, j + 5 - KEYS), second=True)
                if parts < 4 * TT * PH and 5 * (j + 1) // 8 > parts:
                    route_pass(parts // 4, parts % 4)
                    parts += 1
                if j == KEYS - JPB:
                    dve.wait_ge(s_ge, 1)
                    gk = krow[:, 2].rearrange("p t (h k) -> p (t h) k", k=TOPK)
                    gs = stat[:, GS:GS + TT * PH]
                    chain[0] = chain0 + ROUTE_LINKS * TT * PH
                    link(V.tensor_reduce(gs, gk, X, ALU.add))
                    link(V.reciprocal(gs, gs))
                    V.tensor_tensor(gk, gk, gs.unsqueeze(2).broadcast_to([P, TT * PH, TOPK]), ALU.mult).then_inc(s_gr, 1)

            dve.wait_ge(s_kte, 3)
            dve.wait_ge(s_ua, KEYS)

            def equal(dst, key, t0):
                return V.tensor_tensor(dst, iota[:].unsqueeze(1).broadcast_to([P, GRP, P]),
                                       kt3[:, key, ds(t0, GRP)].unsqueeze(2).broadcast_to([P, GRP, P]), ALU.is_equal)

            def onehots(t0, slot):
                equal(oh_i(slot), 0, t0).then_inc(s_oi, 1)
                if slot == 3:
                    equal(oh_j(slot), 1, t0).then_inc(s_ojd, 1)

            def weigh(g, t0, slot):
                dve.wait_ge(s_gm, g + 1)
                aw = act_w[:, :, ds(t0, GRP)]
                V.tensor_tensor(aw, bank[slot][:].rearrange("p (t j) -> p j t", t=GRP), aw, ALU.mult).then_inc(s_gw, 1)

            for slot in range(4):
                onehots(GRP * slot, slot)
            with dve.Fori(0, T // GRP // 4 - 1) as it:
                for slot in range(4):
                    weigh(it * 4 + slot, it * (4 * GRP) + GRP * slot, slot)
                    onehots(it * (4 * GRP) + GRP * (slot + 4), slot)
            for slot in range(4):
                g = T // GRP - 4 + slot
                weigh(g, GRP * g, slot)

            def a_low(j, slot):
                dve.wait_ge(s_Wh, j + 1)
                V.tensor_tensor(whl[:, slot, 1], act_w[:, ds(j, 1)].rearrange("p o t -> p (o t)"), whl[:, slot, 0].bitcast(F32),
                                ALU.subtract).then_inc(s_Wl, 1)

            for k in range(4):
                a_low(k, k)
            split_low(3, s_vl, (s_vh, 4), second=True)
            with dve.Fori(0, KEYS // 4 - 1) as it:
                for k in range(4):
                    split_low(k, s_vl, (s_vh, it * 4 + (k + 5)), second=True)
                    a_low(it * 4 + (k + 4), k)
            dve.wait_ge(s_gf, 16)
            for t in range(TT):
                dve.wait_ge(s_fs, t + 1)
                V.tensor_scalar(stat[:, SS + t:SS + t + 1], stat[:, SS + t:SS + t + 1], 1.0 / D, EPS, ALU.mult, ALU.add).then_inc(s_fv, 1)
                dve.wait_ge(s_fd, t + 1)
                link(V.reciprocal(stat[:, RS + t:RS + t + 1], stat[:, RS + t:RS + t + 1]))
                for n in range(2):
                    V.scalar_tensor_tensor(fin[:, t, 512 * n:512 * n + 512], acc[:, 2 * t + n, :], stat[:, RS + t:RS + t + 1],
                                           gfin[:, 512 * n:512 * n + 512], ALU.mult, ALU.mult).then_inc(s_fin, 1)

        @block.tensor
        def _(pe):
            def transposes(n, src):
                for t in range(TT):
                    pe.wait_ge(s_xs, TT * n + t + 1)
                    for c in range(DC):
                        o = T * (c % 2) + P * t
                        last = pe.transpose(bank[c // 2][:, o:o + P], src[:, t, P * c:P * c + P], ident[:])
                        if t == 1 and c % 2:
                            last.then_inc(s_tr, 1)

            def unit(u, xin, fresh=None, part=(0, DC)):
                if u == 0:
                    pe.wait_ge(s_w0l, 1)
                elif part[0] == 0:
                    wsplit(pe, u)
                    if u >= 2:
                        wevac(pe, u - 2)
                kind = UNITS[u][2]
                wh, wl = wsp[:, u % 2, 0], wsp[:, u % 2, 1]
                for k in range(2):
                    q = slice(P * k, P * k + P)
                    groups = ((0, LC), (LC, DC)) if kind == "groups" else ((0, DC),)
                    for g, (c0, c1) in enumerate(groups):
                        dst = acc[:, 2 * (u % 2) + k, WCOL * g:WCOL * g + WCOL]
                        for c in range(max(c0, part[0]), min(c1, part[1])):
                            if u == 0 and k == 0 and c == 4:
                                pe.wait_ge(s_wl, 1)
                            if fresh and k == 0:
                                pe.wait_ge(fresh[0], fresh[1] + c + 1)
                            if kind == "cols":
                                ops = ((wh[:, c, q], xin[:, c, 0]), (wh[:, c, q], xin[:, c, 1]), (wl[:, c, q], xin[:, c, 0]))
                            else:
                                ops = ((xin[:, c, 0, q], wh[:, c]), (xin[:, c, 0, q], wl[:, c]), (xin[:, c, 1, q], wh[:, c]))
                            for n, (a, b) in enumerate(ops):
                                last = pe.matmul(dst, a, b, start=(c == c0 and n == 0), stop=(c == c1 - 1 and n == 2))
                    if k == 0 and u in (U_CQ - 1, U_PQ - 1):
                        last.then_inc(s_t0, 1)
                if part[1] == DC:
                    last.then_inc(s_wmm, 1)

            def scores(h):
                half = slice(64 * (h % 2), 64 * (h % 2) + 64)
                b = bank[SCB + h % 2]
                if h >= 2:
                    pe.wait_ge(s_mx, h - 1)
                pe.matmul(b[:, 0:P], qt[half, h // 2, 0:P], ktt[half, h // 2, 0:P], start=True, stop=True)
                pe.matmul(b[:, P:3 * P], qt[half, h // 2, P:2 * P], ktt[half, h // 2, :], start=True, stop=True).then_inc(s_sc, 1)

            def probs_t(h):
                pe.wait_ge(s_pn, h + 1)
                if h >= 1:
                    pe.wait_ge(s_pe, h)
                p = pbuf[:, h % 2]
                pe.transpose(bank[TRB][:, 0:P], p[:, 0:P], ident[:])
                pe.transpose(bank[TRB][:, P:2 * P], p[:, P:2 * P], ident[:])
                pe.transpose(bank[TRB][:, 2 * P:3 * P], p[:, 2 * P:3 * P], ident[:]).then_inc(s_pt, 1)

            def head_pv(h):
                half = slice(64 * (h % 2), 64 * (h % 2) + 64)
                pe.wait_ge(s_pe, h + 1)
                if h >= 1:
                    pe.wait_ge(s_pve, h)
                vh = slice(DH * h, DH * h + DH)
                pe.matmul(bank[OUB][half, 0:T], v_sb[:, 0, vh], ptr[:, h % 2, 0:T], start=True, stop=False)
                pe.matmul(bank[OUB][half, P:T], v_sb[:, 1, vh], ptr[:, h % 2, T:T + P], start=False, stop=True).then_inc(s_pv, 1)

            pe.wait_ge(s_const, 7)
            transposes(0, xs)
            unit(0, xt, (s_tl, 0))
            unit(1, xt)
            transposes(1, mr)
            unit(2, xt)
            unit(3, xt)
            pe.wait_ge(s_bd, 64)
            pe.wait_ge(s_cv, CONV * LC)
            pe.wait_ge(s_tl, 2 * DC)
            for mch in range(LC):
                pe.matmul(bank[mch][:, 0:T], bd[:, 0, mch], cv_[:, mch], start=True, stop=True)
                pe.matmul(bank[mch][:, T:2 * T], bd[:, 1, mch], cv_[:, mch], start=True, stop=True).then_inc(s_lg, 1)
            for u in range(4, 9):
                unit(u, xt)
            wevac(pe, U_K + 1)
            pe.wait_ge(s_sg, LC)
            scores(0)
            for h in range(HEADS):
                if h + 1 < HEADS:
                    scores(h + 1)
                if h == 0:
                    unit(U_V + 1, xt)
                else:
                    unit(9 + h, memt)
                probs_t(h)
                if h == 1:
                    wevac(pe, U_V + 1)
                if h:
                    head_pv(h - 1)
            unit(U_OUT - 1, memt)
            head_pv(HEADS - 1)
            unit(U_OUT, mixt, (s_gl, 0))
            pe.wait_ge(s_gad, 6)
            for g, sq in enumerate((r_, i_)):
                for t in range(TT):
                    last = pe.matmul(bank[OUB][:, T + 2 * g + t:T + 2 * g + t + 1], sq[:, 0, P * t:P * t + P], ones[:, 0:1],
                                     start=True, stop=True)
            last.then_inc(s_gmm, 1)
            for u in range(U_OUT + 1, U_CQ):
                unit(u, mixt)
            transposes(2, xs)

            def cross_scores(h):
                n = HEADS + h
                b = bank[SCB + n % 2]
                pe.wait_ge(s_ex, n - 1)
                for t in range(TT):
                    for c in range(2):
                        last = pe.matmul(b[:, T * t:T * t + T], qct[:, 2 * h + c, P * t:P * t + P], kct[:, 2 * h + c, :],
                                         start=(c == 0), stop=(c == 1))
                last.then_inc(s_sc, 1)

            def cross_probs_t(h):
                n = HEADS + h
                pe.wait_ge(s_pn, n + 1)
                pe.wait_ge(s_pe, n)
                for t in range(TT):
                    for k in range(TT):
                        last = pe.transpose(bank[TRB][:, T * k + P * t:T * k + P * t + P], pbuf[:, n % 2, T * t + P * k:T * t + P * k + P],
                                            ident[:])
                last.then_inc(s_pt, 1)

            def cross_pv(h):
                n = HEADS + h
                pe.wait_ge(s_pe, n + 1)
                if h:
                    pe.wait_ge(s_cl, h)
                for c in range(2):
                    for k in range(TT):
                        d0 = CDH * h + P * c
                        last = pe.matmul(bank[OUB][:, T * c:T * c + T], vc[:, k, d0:d0 + P], ptr[:, n % 2, T * k:T * k + T],
                                         start=(k == 0), stop=(k == TT - 1))
                last.then_inc(s_pv, 1)

            unit(U_CQ, xt, (s_tl, 2 * DC))
            unit(U_CQ + 1, xt)
            wevac(pe, U_CQ)
            cross_scores(0)
            unit(U_CQ + 2, xt)
            wevac(pe, U_CQ + 1)
            cross_scores(1)
            cross_probs_t(0)
            unit(U_CQ + 3, xt)
            cross_pv(0)
            cross_probs_t(1)
            wevac(pe, U_CQ + 3)
            cross_scores(2)
            cross_pv(1)
            cross_scores(3)
            cross_probs_t(2)
            pe.wait_ge(s_cl, 2)
            unit(U_CO, oct_, part=(0, 2))
            cross_pv(2)
            cross_probs_t(3)
            unit(U_CO, oct_, part=(2, 4))
            cross_pv(3)
            unit(U_CO, oct_, part=(4, 6))
            pe.wait_ge(s_cl, 4)
            unit(U_CO, oct_, part=(6, 8))
            for u in range(U_CO + 1, U_PQ):
                unit(u, oct_)
            transposes(3, xs)
            unit(U_PQ, xt, (s_tl, 3 * DC))
            for u in range(U_PQ + 1, NU):
                unit(u, xt)
            pe.wait_ge(s_keys, 16)
            wevac(pe, NU - 1)
            for t in range(TT):
                for b in range(4):
                    n = 4 * t + b
                    if n >= 4:
                        pe.wait_ge(s_ke, n - 3)
                    for k in range(4):
                        hp = 4 * b + k
                        last = pe.matmul(bank[b][:, P * k:P * k + P], qpt[:, hp, P * t:P * t + P], keys[:, hp], start=True, stop=True)
                    last.then_inc(s_ks, 1)

            for t in range(TT):
                for n in range(2):
                    last = pe.matmul(acc[:, 2 * t + n], ident[:], xr[:, t, 512 * n:512 * n + 512], start=True, stop=False,
                                     skip_group_check=True)
            last.then_inc(s_seed, 1)

            def u_keys(it, first=False, last_pass=False):
                for k in range(4):
                    pe.wait_ge(s_ul, it * 4 + (k + 1))
                    if first:
                        pe.wait_ge(s_ke, 5 + k)
                    else:
                        pe.wait_ge(s_ua, it * 4 + (k - 3))
                    uh = eslot(k, 0, False).rearrange("p (c i) -> p c i", c=DC)
                    ul = eslot(k, 1, False).rearrange("p (c i) -> p c i", c=DC)
                    for c in range(DC):
                        pe.matmul(bank[k][:, 0:T], uh[:, c], xt[:, c, 0], start=(c == 0), stop=False)
                        pe.matmul(bank[k][:, 0:T], uh[:, c], xt[:, c, 1], start=False, stop=False)
                        last = pe.matmul(bank[k][:, 0:T], ul[:, c], xt[:, c, 0], start=False, stop=(c == DC - 1))
                    if last_pass and k < 3:
                        if k == 0:
                            pe.wait_ge(s_gr, 1)
                        for t in range(TT):
                            last = pe.transpose(bank[k][:, T + P * t:T + P * t + P], krow[:, k, t], ident[:])
                    last.then_inc(s_um, 1)

            u_keys(0, first=True)
            with pe.Fori(1, KEYS // 4 - 1) as it:
                u_keys(it)
            u_keys(KEYS // 4 - 1, last_pass=True)

            pe.wait_ge(s_ua, KEYS)
            pe.wait_ge(s_kte, 3)

            def route(it, slot, first=False):
                pe.wait_ge(s_gi, it * 4 + (slot + 1))
                if slot == 3:
                    pe.wait_ge(s_ojd, it + 1)
                else:
                    pe.wait_ge(s_oja, it * 3 + (slot + 1))
                if not first:
                    pe.wait_ge(s_gw, it * 4 + (slot - 3))
                for k in range(GRP):
                    last = pe.matmul(bank[slot][:, P * k:P * k + P], oh_i(slot)[:, k], oh_j(slot)[:, k], start=True, stop=True)
                last.then_inc(s_gm, 1)

            for slot in range(4):
                route(0, slot, first=True)
            with pe.Fori(1, T // GRP // 4) as it:
                for slot in range(4):
                    route(it, slot)

            def v_key(j, slot, last_key=False):
                pe.wait_ge(s_vl, j + 1)
                pe.wait_ge(s_Wl, j + 1)
                vh, vl = eslot(slot, 0, True), eslot(slot, 1, True)
                for t in range(TT):
                    ah, al = whl[:, slot, 0, P * t:P * t + P], whl[:, slot, 1, P * t:P * t + P]
                    for k, (a, b) in enumerate(((ah, vh), (ah, vl), (al, vh))):
                        for n in range(2):
                            last = pe.matmul(acc[:, 2 * t + n], a, b[:, 512 * n:512 * n + 512], start=False,
                                             stop=last_key and k == 2, skip_group_check=True)
                    if last_key and t == 0:
                        last.then_inc(s_yt, 1)
                last.then_inc(s_vm, 1)

            with pe.Fori(0, KEYS // 4 - 1) as it:
                for slot in range(4):
                    v_key(it * 4 + slot, slot)
            for slot in range(4):
                v_key(KEYS - 4 + slot, slot, last_key=slot == 3)


def kernel(**inputs):
    import numpy as np
    import concourse.bacc as bacc
    from concourse.bass_utils import run_bass_kernel_spmd as run

    def chunks(a, n):
        return np.asarray(a).reshape(-1, n, P).transpose(2, 0, 1).reshape(P, -1)

    i = {k: np.asarray(a) for k, a in inputs.items()}
    par = np.concatenate([
        chunks(i["ln_mix_g"][0], DC), chunks(i["ln_mem_g"][0], DC), chunks(i["ln_cross_g"][0], DC), chunks(i["ln_ffn_g"][0], DC),
        chunks(i["gn_lru_g"][0], LC), chunks(i["gn_attn_g"][0], LC), chunks(i["conv_w"][0], LC), chunks(i["conv_b"][0], LC),
        chunks(i["lru_ba"][0], LC), chunks(i["lru_bx"][0], LC), chunks(i["lru_lambda"][0], LC)], axis=1)
    u_t = i["peer_u"][0].reshape(KEYS, KEYS // 2, 2, DC, P).transpose(1, 4, 2, 3, 0).reshape(KEYS // 2, P, 2, D)
    keys_t = i["peer_subkeys"][0].reshape(2 * PH, KEYS, P).transpose(2, 0, 1)
    arrays = {
        "x": i["x"][0], "mem": i["mem"][0], "par": par, "wa": i["lru_wa"][0], "wx": i["lru_wx"][0],
        "w_in": i["w_in"][0], "w_ck": i["w_ck"][0], "w_cv": i["w_cv"][0], "w_out": i["w_out"][0], "w_cq": i["w_cq"][0],
        "w_co": i["w_co"][0], "w_pq": i["peer_wq"][0], "keys_t": keys_t, "u_t": u_t, "v": i["peer_v"][0],
        "g_final": i["ln_final_g"],
    }
    arrays = {k: np.ascontiguousarray(a) for k, a in arrays.items()}
    nc = bacc.Bacc("TRN2", target_bir_lowering=False, num_devices=1)
    ap = {k: nc.dram_tensor(k, a.shape, mybir.dt.from_np(a.dtype), kind="ExternalInput").ap() for k, a in arrays.items()}
    out = nc.dram_tensor("out", (T, D), F32, kind="ExternalOutput").ap()
    w = {k: ap[k] for k in ("w_in", "w_ck", "w_cv", "w_out", "w_cq", "w_co", "w_pq")}
    build(nc, ap["x"], ap["mem"], ap["par"], ap["wa"], ap["wx"], w, ap["keys_t"], ap["u_t"], ap["v"], ap["g_final"], out)
    r = run(nc, [arrays], core_ids=[0])
    return r.results[0]["out"].reshape(1, T, D)
```
